# Optimizing a Trainium2 kernel written in Bass

```python
import jax, jax.numpy as jnp
from jax import lax
import numpy as np

D_MODEL = 1024
BATCH = 1
SEQ = 1024
DEPTH = 1
DEC_BATCH = 8
DEC_SEQ = 8
PAST_LEN = 8192
PAGE_SIZE = 128

RET_HEADS = 8
RET_DK = 64
RET_DV = D_MODEL // RET_HEADS
RET_CHUNK = 128
ROPE_BASE = 10000.0
LRU_WIDTH = D_MODEL
LRU_BLOCKS = 16
LRU_BW = LRU_WIDTH // LRU_BLOCKS
CONV_W = 4
LRU_C = 8.0
PEER_HEADS = 8
PEER_NKEYS = 128
PEER_N = PEER_NKEYS * PEER_NKEYS
PEER_DKEY = 256
PEER_HALF = PEER_DKEY // 2
PEER_TOPK = 16
PEER_BLOCK = 128
Q_W = RET_HEADS * RET_DK
V_W = RET_HEADS * RET_DV
IN_WIDTH = 2 * Q_W + 2 * V_W + 2 * LRU_WIDTH + 2 * D_MODEL
EPS = 1e-6

kernel_name = "hybrid_retention_rglru_peer_adaln_step"

F32 = jnp.float32

def rmsnorm(x, w):
    xf = x.astype(F32)
    y = xf * lax.rsqrt(jnp.mean(xf * xf, axis=-1, keepdims=True) + EPS)
    return (y * w.astype(F32)).astype(x.dtype)

def rope(t, pos):
    half = t.shape[-1] // 2
    inv = jnp.power(ROPE_BASE, -jnp.arange(half, dtype=F32) / half)
    ang = pos.astype(F32)[:, None] * inv[None, :]
    cos = jnp.cos(ang)[None, :, None, :]
    sin = jnp.sin(ang)[None, :, None, :]
    t1 = t[..., :half].astype(F32)
    t2 = t[..., half:].astype(F32)
    return jnp.concatenate([t1 * cos - t2 * sin, t1 * sin + t2 * cos], axis=-1)

def retention(q, k, v, S0):
    B, L, H, _ = q.shape
    dv = v.shape[-1]
    C = RET_CHUNK if L % RET_CHUNK == 0 else L
    nc = L // C
    log_g = jnp.log1p(-jnp.exp2(-5.0 - jnp.arange(H, dtype=F32)))
    idx = jnp.arange(C, dtype=F32)
    diff = idx[:, None] - idx[None, :]
    mask = jnp.where(diff[None] >= 0, jnp.exp(jnp.maximum(diff, 0.0)[None] * log_g[:, None, None]), 0.0)
    xi = jnp.exp((idx[:, None] + 1.0) * log_g[None, :])
    zeta = jnp.exp((C - 1.0 - idx[:, None]) * log_g[None, :])
    g_chunk = jnp.exp(C * log_g)

    def to_chunks(t):
        return t.astype(F32).reshape(B, nc, C, H, t.shape[-1]).transpose(1, 0, 2, 3, 4)

    def step(S, inp):
        qc, kc, vc = inp
        scores = jnp.einsum('bnhd,bmhd->bhnm', qc, kc) * mask
        o = (jnp.einsum('bhnm,bmhv->bnhv', scores, vc)
             + jnp.einsum('bnhd,bhdv->bnhv', qc, S) * xi[None, :, :, None])
        S = S * g_chunk[None, :, None, None] + jnp.einsum('bmhd,bmhv->bhdv', kc * zeta[None, :, :, None], vc)
        return S, o

    S, o = lax.scan(step, S0.astype(F32), (to_chunks(q), to_chunks(k), to_chunks(v)))
    o = o.transpose(1, 0, 2, 3, 4).reshape(B, L, H, dv)
    return o, S

def head_groupnorm(o, w):
    B, L = o.shape[:2]
    mean = jnp.mean(o, axis=-1, keepdims=True)
    var = jnp.mean(jnp.square(o - mean), axis=-1, keepdims=True)
    y = (o - mean) * lax.rsqrt(var + EPS)
    return y.reshape(B, L, -1) * w.astype(F32)

def causal_conv(x, buf, w, b):
    L = x.shape[1]
    xp = jnp.concatenate([buf.astype(x.dtype), x], axis=1)
    y = b + sum(xp[:, j:j + L] * w[j] for j in range(CONV_W))
    return y, xp[:, L:]

def rg_lru(xl, h0, w_a, b_a, w_x, b_x, lam):
    B, L, W = xl.shape
    xb = xl.reshape(B, L, LRU_BLOCKS, LRU_BW)
    r = jax.nn.sigmoid(jnp.einsum('blnd,nde->blne', xb, w_a).reshape(B, L, W) + b_a)
    i = jax.nn.sigmoid(jnp.einsum('blnd,nde->blne', xb, w_x).reshape(B, L, W) + b_x)
    log_a = (-LRU_C * jax.nn.softplus(-lam.astype(F32))) * r.astype(F32)
    a = jnp.exp(log_a)
    mult = jnp.sqrt(-jnp.expm1(2.0 * log_a))
    bterm = mult * (i * xl).astype(F32)
    bterm = bterm.at[:, 0].add(a[:, 0] * h0.astype(F32))

    def combine(e1, e2):
        a1, b1 = e1
        a2, b2 = e2
        return a1 * a2, a2 * b1 + b2

    _, h = lax.associative_scan(combine, (a, bterm), axis=1)
    return h.astype(xl.dtype), h[:, -1]

def peer(x, w_q, k1, k2, u_tab, v_tab):
    B, L, D = x.shape
    T = B * L
    xf = x.reshape(T, D)
    q = (xf @ w_q).reshape(T, PEER_HEADS, PEER_DKEY)
    s1 = jnp.einsum('thd,nd->thn', q[..., :PEER_HALF], k1).astype(F32)
    s2 = jnp.einsum('thd,nd->thn', q[..., PEER_HALF:], k2).astype(F32)
    v1, i1 = lax.top_k(s1, PEER_TOPK)
    v2, i2 = lax.top_k(s2, PEER_TOPK)
    cand = (v1[..., :, None] + v2[..., None, :]).reshape(T, PEER_HEADS, PEER_TOPK * PEER_TOPK)
    sc, pidx = lax.top_k(cand, PEER_TOPK)
    e1 = jnp.take_along_axis(i1, pidx // PEER_TOPK, axis=-1)
    e2 = jnp.take_along_axis(i2, pidx % PEER_TOPK, axis=-1)
    n_sel = PEER_HEADS * PEER_TOPK
    expert = (e1 * PEER_NKEYS + e2).reshape(T, n_sel)
    g = jax.nn.softmax(sc, axis=-1).reshape(T, n_sel).astype(x.dtype)
    n_blk = -(-T // PEER_BLOCK)
    pad = n_blk * PEER_BLOCK - T
    if pad > 0:
        xf = jnp.pad(xf, ((0, pad), (0, 0)))
        expert = jnp.pad(expert, ((0, pad), (0, 0)))
        g = jnp.pad(g, ((0, pad), (0, 0)))

    def blk(args):
        xb, eb, gb = args
        act = jax.nn.gelu(jnp.einsum('td,tkd->tk', xb, u_tab[eb]))
        return jnp.einsum('tk,tkd->td', gb * act, v_tab[eb])

    out = lax.map(blk, (xf.reshape(n_blk, PEER_BLOCK, D),
                        expert.reshape(n_blk, PEER_BLOCK, n_sel),
                        g.reshape(n_blk, PEER_BLOCK, n_sel)))
    return out.reshape(n_blk * PEER_BLOCK, D)[:T].reshape(B, L, D)

def layer(x, c, S0, h0, conv0, pos_offset, w_ada, b_ada, norm1_w, w_in, ret_gn_w, conv_w, conv_b,
          lru_wa, lru_ba, lru_wx, lru_bx, lru_lambda, w_out, norm2_w, peer_wq, peer_k1, peer_k2,
          peer_u, peer_v):
    B, L, _ = x.shape
    mod = jax.nn.silu(c) @ w_ada + b_ada
    sh1, sc1, g1, sh2, sc2, g2 = jnp.split(mod[:, None, :], 6, axis=-1)
    hn = rmsnorm(x, norm1_w) * (1.0 + sc1) + sh1
    proj = hn @ w_in
    widths = [Q_W, Q_W, V_W, V_W, LRU_WIDTH, LRU_WIDTH, D_MODEL, D_MODEL]
    points, acc = [], 0
    for wdt in widths[:-1]:
        acc += wdt
        points.append(acc)
    q, k, v, g_ret, x_lru, g_lru, gate_a, gate_b = jnp.split(proj, points, axis=-1)
    pos = jnp.arange(L, dtype=jnp.int32) + pos_offset
    q = rope(q.reshape(B, L, RET_HEADS, RET_DK), pos)
    k = rope(k.reshape(B, L, RET_HEADS, RET_DK), pos) * (RET_DK ** -0.5)
    o, S = retention(q, k, v.reshape(B, L, RET_HEADS, RET_DV), S0)
    ret_out = jax.nn.silu(g_ret) * head_groupnorm(o, ret_gn_w).astype(x.dtype)
    xl, conv_new = causal_conv(x_lru, conv0, conv_w, conv_b)
    hseq, h_last = rg_lru(xl, h0, lru_wa, lru_ba, lru_wx, lru_bx, lru_lambda)
    lru_out = hseq * jax.nn.gelu(g_lru)
    merged = jax.nn.sigmoid(gate_a) * ret_out + jax.nn.sigmoid(gate_b) * lru_out
    x = x + g1 * (merged @ w_out)
    hn2 = rmsnorm(x, norm2_w) * (1.0 + sc2) + sh2
    x = x + g2 * peer(hn2, peer_wq, peer_k1, peer_k2, peer_u, peer_v)
    return x, S, h_last, conv_new

def run_group(x, c, S0, h0, conv0, pos_offset, layer_weights, final_norm_w):
    Ss, hs, cs = [], [], []
    for l in range(DEPTH):
        x, S, h, cb = layer(x, c, S0[l], h0[l], conv0[l], pos_offset, *[w[l] for w in layer_weights])
        Ss.append(S.astype(x.dtype))
        hs.append(h.astype(x.dtype))
        cs.append(cb.astype(x.dtype))
    return rmsnorm(x, final_norm_w), jnp.stack(Ss), jnp.stack(hs), jnp.stack(cs)

def setup_inputs(seed: int = 0) -> dict:
    key = jax.random.key(seed)
    ks = jax.random.split(key, 32)
    nrm = lambda k, shape, s: jax.random.normal(k, shape, F32) * s
    gain = lambda k, shape: 1.0 + 0.05 * jax.random.normal(k, shape, F32)
    a0 = jax.random.uniform(ks[17], (DEPTH, LRU_WIDTH), F32, minval=0.9, maxval=0.999)
    return {
        "x_prompt": nrm(ks[0], (BATCH, SEQ, D_MODEL), 1.0),
        "x_sample": nrm(ks[1], (DEC_BATCH, DEC_SEQ, D_MODEL), 1.0),
        "c_prompt": nrm(ks[2], (BATCH, D_MODEL), 1.0),
        "c_sample": nrm(ks[3], (DEC_BATCH, D_MODEL), 1.0),
        "state_ret": nrm(ks[4], (DEPTH, DEC_BATCH, RET_HEADS, RET_DK, RET_DV), 0.5),
        "state_lru": nrm(ks[5], (DEPTH, DEC_BATCH, LRU_WIDTH), 0.5),
        "state_conv": nrm(ks[6], (DEPTH, DEC_BATCH, CONV_W - 1, LRU_WIDTH), 1.0),
        "w_ada": nrm(ks[7], (DEPTH, D_MODEL, 6 * D_MODEL), 0.5 * D_MODEL ** -0.5),
        "b_ada": nrm(ks[8], (DEPTH, 6 * D_MODEL), 0.01),
        "norm1_w": gain(ks[9], (DEPTH, D_MODEL)),
        "w_in": nrm(ks[10], (DEPTH, D_MODEL, IN_WIDTH), D_MODEL ** -0.5),
        "ret_gn_w": gain(ks[11], (DEPTH, V_W)),
        "conv_w": nrm(ks[12], (DEPTH, CONV_W, LRU_WIDTH), CONV_W ** -0.5),
        "conv_b": nrm(ks[13], (DEPTH, LRU_WIDTH), 0.01),
        "lru_wa": nrm(ks[14], (DEPTH, LRU_BLOCKS, LRU_BW, LRU_BW), LRU_BW ** -0.5),
        "lru_ba": nrm(ks[15], (DEPTH, LRU_WIDTH), 0.01),
        "lru_wx": nrm(ks[16], (DEPTH, LRU_BLOCKS, LRU_BW, LRU_BW), LRU_BW ** -0.5),
        "lru_bx": nrm(ks[18], (DEPTH, LRU_WIDTH), 0.01),
        "lru_lambda": jnp.log(a0) - jnp.log1p(-a0),
        "w_out": nrm(ks[19], (DEPTH, D_MODEL, D_MODEL), D_MODEL ** -0.5),
        "norm2_w": gain(ks[20], (DEPTH, D_MODEL)),
        "peer_wq": nrm(ks[21], (DEPTH, D_MODEL, PEER_HEADS * PEER_DKEY), D_MODEL ** -0.5),
        "peer_k1": nrm(ks[22], (DEPTH, PEER_NKEYS, PEER_HALF), PEER_HALF ** -0.5),
        "peer_k2": nrm(ks[23], (DEPTH, PEER_NKEYS, PEER_HALF), PEER_HALF ** -0.5),
        "peer_u": nrm(ks[24], (DEPTH, PEER_N, D_MODEL), D_MODEL ** -0.5),
        "peer_v": nrm(ks[25], (DEPTH, PEER_N, D_MODEL), 1.0),
        "final_norm_w": gain(ks[26], (D_MODEL,)),
    }

def reference(x_prompt, x_sample, c_prompt, c_sample, state_ret, state_lru, state_conv, w_ada, b_ada,
              norm1_w, w_in, ret_gn_w, conv_w, conv_b, lru_wa, lru_ba, lru_wx, lru_bx, lru_lambda,
              w_out, norm2_w, peer_wq, peer_k1, peer_k2, peer_u, peer_v, final_norm_w):
    layer_weights = (w_ada, b_ada, norm1_w, w_in, ret_gn_w, conv_w, conv_b, lru_wa, lru_ba, lru_wx,
                     lru_bx, lru_lambda, w_out, norm2_w, peer_wq, peer_k1, peer_k2, peer_u, peer_v)
    dt = x_prompt.dtype
    S0_p = jnp.zeros((DEPTH, BATCH, RET_HEADS, RET_DK, RET_DV), dt)
    h0_p = jnp.zeros((DEPTH, BATCH, LRU_WIDTH), dt)
    conv0_p = jnp.zeros((DEPTH, BATCH, CONV_W - 1, LRU_WIDTH), dt)
    y_prompt, ret_prompt, lru_prompt, conv_prompt = run_group(
        x_prompt, c_prompt, S0_p, h0_p, conv0_p, 0, layer_weights, final_norm_w)
    y_sample, ret_sample, lru_sample, conv_sample = run_group(
        x_sample, c_sample, state_ret, state_lru, state_conv, PAST_LEN, layer_weights, final_norm_w)
    return (y_prompt, y_sample, ret_prompt, lru_prompt, conv_prompt, ret_sample, lru_sample, conv_sample)


_drawn_inputs = setup_inputs


def setup_inputs(seed=0):
    import zlib

    import numpy as np

    out = dict(_drawn_inputs(seed))
    spreads = {}
    factors = {'ret_gn_w': 3.738, 'lru_ba': 24.815, 'lru_bx': 8.0}
    for name, (base, spread) in spreads.items():
        noise = np.random.default_rng([zlib.crc32(name.encode()), seed]).standard_normal(out[name].shape)
        drawn = base * np.exp(spread * noise) if base else spread * noise
        out[name] = __import__('jax').numpy.asarray(drawn.astype(out[name].dtype))
    for name, factor in factors.items():
        out[name] = (out[name] * factor).astype(out[name].dtype)
    return out
```

```python
from contextlib import ExitStack

import numpy as np
import concourse.bass as bass
from concourse import mybir

F32 = mybir.dt.float32
U32 = mybir.dt.uint32
ALU = mybir.AluOpType
ACT = mybir.ActivationFunctionType
AX = mybir.AxisListType.X

P = 128
D = 1024
KC = D // P
SEQ = 1024
NB, NS = 8, 8
TS = NB * NS
T = SEQ + TS
NT = SEQ // P + 1
TPAD = NT * P
H = 8
DK = 64
CONV = 4
HIST = CONV - 1
XR = HIST + SEQ
CW = DK + DK + P
SLAB = CW + 5 * P
TOPK = 16
NKEY = 128
EPS = 1e-6
PAST = 8192
SLICES = ((0, 512), (512, 1024), (1024, T))
STAIRS = ((0, 1, 16, 0), (1, 1, 8, 16), (2, 2, 5, 24), (4, 4, 3, 34), (8, 8, 1, 46))
NCAND = 54
ADA_W = 512
ADA_CH = ADA_W // P
NMOD = 40
SH1, SC1, G1, SH2, SC2 = 0, 8, 16, 24, 32
V_N1, V_N2, V_GN, V_CB, V_CW, V_BA, V_BX, V_LAM, NVEC = 0, 1, 2, 3, 4, 8, 9, 10, 11
RING = 8
LOW = -3.0e38


def tables():
    t = np.zeros((TPAD,), np.float32)
    t[:SEQ] = np.arange(SEQ)
    t[SEQ:T] = PAST + np.arange(TS) % NS
    half = DK // 2
    inv = np.power(np.float32(10000.0), -np.arange(half, dtype=np.float32) / np.float32(half)).astype(np.float32)
    ang = (t[:, None] * inv[None]).astype(np.float32).astype(np.float64)
    cos, sin = np.cos(ang), np.sin(ang)
    rope_c = np.concatenate([cos, cos], 1).reshape(NT, P, DK).transpose(1, 0, 2)
    rope_s = np.concatenate([-sin, sin], 1).reshape(NT, P, DK).transpose(1, 0, 2)
    lg = np.log1p(-np.exp2(-5.0 - np.arange(H)))
    n = np.arange(P)
    diff = n[None, :] - n[:, None]
    mask = np.where(diff[None] >= 0, np.exp(np.maximum(diff, 0)[None] * lg[:, None, None]), 0.0)
    m = np.arange(TS)
    sdiff = m[None, :] - m[:, None]
    same = (m[None, :] // NS == m[:, None] // NS) & (sdiff >= 0)
    smask = np.where(same[None], np.exp(np.maximum(sdiff, 0)[None] * lg[:, None, None]), 0.0)
    xi = np.exp((n[None, :] + 1.0) * lg[:, None])
    scale = DK ** -0.5
    zeta = np.exp((P - 1.0 - n[:, None]) * lg[None]) * scale
    szeta = np.exp((NS - 1.0 - (m % NS)[:, None, None]) * lg[None, :, None]) * scale
    szeta = szeta * (m[:, None, None] // NS == np.arange(NB)[None, None, :])
    gch = np.stack([np.exp(P * lg), np.exp(NS * lg)])
    c = {
        "rope_c": rope_c, "rope_s": rope_s,
        "dmask": mask.transpose(1, 0, 2), "smask": smask.transpose(1, 0, 2),
        "xi": np.broadcast_to(xi[None], (DK, H, P)),
        "zeta": zeta, "szeta": szeta,
        "gch": np.broadcast_to(gch[None], (DK, 2, H)),
        "ident": np.eye(P),
        "iota": np.broadcast_to(np.arange(NCAND)[None], (P, NCAND)),
    }
    return {k: np.ascontiguousarray(v, dtype=np.float32) for k, v in c.items()}


class Chain:

    def __init__(self, eng, sem):
        self.eng, self.sem, self.base, self.k, self.off = eng, sem, 0, 0, None

    def __call__(self, ins):
        self.k += 1
        ins.then_inc(self.sem, 1)
        at = self.base + self.k
        self.eng.wait_ge(self.sem, at if self.off is None else self.off + at)

    def loop(self, i, per):
        self.flat()
        self.off, self.per = i * per, per

    def end(self, n):
        assert self.k == self.per, f"{self.k} links in the loop's body"
        self.base, self.k, self.off = self.base + n * self.per, 0, None

    def flat(self):
        self.base, self.k = self.base + self.k, 0


def program(nc, I, O, S):
    ctx = ExitStack()

    def sem(name):
        return ctx.enter_context(nc.semaphore(name))

    def sb(c, name, shape, dt=F32):
        return c.enter_context(nc.sbuf_tensor(name, shape, dt))

    def bc(ap, axis, shape):
        return ap.unsqueeze(axis).broadcast_to(shape)

    hold_sem = sem("hold")

    def hold(eng):
        eng.sem_inc(hold_sem, 1)

    with ctx:
        pj = ctx.enter_context(nc.psum_tensor("pj", [P, 1536], F32))
        pk = ctx.enter_context(nc.psum_tensor("pk", [P, 1536], F32))
        R = [ctx.enter_context(nc.psum_tensor(f"r{i}", [P, 512], F32)) for i in range(2)]

        dve_chain, act_chain, pool_chain = sem("dve_chain"), sem("act_chain"), sem("pool_chain")
        dl_ = Chain(nc.vector, dve_chain)
        al_ = Chain(nc.scalar, act_chain)
        gl_ = Chain(nc.gpsimd, pool_chain)

        vec = sb(ctx, "vec", [P, NVEC, KC])
        modT = sb(ctx, "modT", [P, NMOD, 1 + NB])
        ones = sb(ctx, "ones", [P, P])
        onesm = sb(ctx, "onesm", [P, P])
        coef = sb(ctx, "coef", [P, KC])
        ident = sb(ctx, "ident", [P, P])
        eidx = sb(ctx, "eidx", [P, NT, P], U32)
        gw = sb(ctx, "gw", [P, NT, H, TOPK])
        epsb = sb(ctx, "epsb", [P, 1])

        mix = ExitStack()
        hnT = sb(mix, "hnT", [P, KC, TPAD])
        w_qkv = sb(mix, "w_qkv", [P, KC, CW])
        w_part = [sb(mix, f"w_part{j}", [P, KC, P]) for j in range(5)]
        wab = sb(mix, "wab", [P, 2, P])

        w_in_sems = [sem(f"w_in{j}") for j in range(6)]
        wab_in = sem("wab_in")

        def adjust(eng_chain, x, out, rstd, gain, shift, tmp):
            v = nc.vector
            for k in range(KC):
                ins = v.scalar_tensor_tensor(out[:, k, 0:SEQ], x[:, k, 0:SEQ], gain[:, k, 0:1], rstd[:, 0:SEQ], ALU.mult, ALU.mult)
            ins2 = v.tensor_tensor(tmp[:, :, :], x[:, :, SEQ:T], bc(rstd[:, SEQ:T], 1, [P, KC, TS]), ALU.mult)
            eng_chain(ins2)
            for k in range(KC):
                v.tensor_scalar(out[:, k, 0:SEQ], out[:, k, 0:SEQ], shift[:, k, 0:1], None, ALU.add)
            t4 = tmp[:, :, :].rearrange("p k (b t) -> p k b t", t=NS)
            o4 = out[:, :, SEQ:T].rearrange("p k (b t) -> p k b t", t=NS)
            eng_chain(v.tensor_tensor(t4, t4, bc(gain[:, :, 1:1 + NB], 3, [P, KC, NB, NS]), ALU.mult))
            eng_chain(v.tensor_tensor(o4, t4, bc(shift[:, :, 1:1 + NB], 3, [P, KC, NB, NS]), ALU.add))

        s0 = ExitStack()
        xT = sb(s0, "xT", [P, KC, T])
        cT = sb(s0, "cT", [P, KC, 1 + NB])
        scT = sb(s0, "scT", [P, KC, 1 + NB])
        rep = sb(s0, "rep", [P, KC, P + TS])
        bada = sb(s0, "bada", [P, 48])
        brow = sb(s0, "brow", [P, D])
        g2b = sb(s0, "g2b", [P, 2, D])
        ada = [sb(s0, f"ada{u}", [P, KC, ADA_W]) for u in range(2)]
        sq = [sb(s0, f"sq{u}", [P, T]) for u in range(2)]
        rstd = sb(s0, "rstd", [P, T])
        gain = sb(s0, "gain", [P, KC, 1 + NB])
        tmp0 = sb(s0, "tmp0", [P, KC, TS])
        lam = [sb(s0, f"lam{i}", [P, KC]) for i in range(5)]

        x_in, small_in, ada_in = sem("x_in"), sem("small_in"), [sem("ada_in0"), sem("ada_in1")]
        ada_used, mod_ps, mod_read = sem("ada_used"), sem("mod_ps"), sem("mod_read")
        sc_ready, rep_ready = sem("sc_ready"), sem("rep_ready")
        sq_ready, sq_used, ssum_ready, sd_ready = sem("sq_ready"), sem("sq_used"), sem("ssum_ready"), sem("sd_ready")
        ones_ready, e_ready, u_ready, ln_ready = sem("ones_ready"), sem("e_ready"), sem("u_ready"), sem("ln_ready")
        g2_ps, g2_ready, g2_out = sem("g2_ps"), sem("g2_ready"), sem("g2_out")

        def w_in_load(sp, f, j):
            a, b = (0, CW) if j == 0 else (CW + (j - 1) * P, CW + j * P)
            dst = w_qkv if j == 0 else w_part[j - 1]
            src = I["w_in"][bass.ds(f, 1), :, a:b].rearrange("o (k p) n -> p (o k) n", p=P)
            sp.dma_start(dst[:, :, :], src).then_inc(w_in_sems[j], 16)

        def wab_load(sp, f):
            for q in range(2):
                src = I["wax"][bass.ds(f, 1), 64 * q:64 * q + 64].rearrange("o p a e -> p (o a) e")
                sp.dma_start(wab[64 * q:64 * q + 64, :, 64 * q:64 * q + 64], src).then_inc(wab_in, 16)

        with nc.Block() as block:
            @block.sync
            def _(sp):
                def ada_load(s, u):
                    sp.dma_start(ada[u][:, :, :], I["w_ada"][:, bass.ts(s, ADA_W)].rearrange("(k p) n -> p k n", p=P)).then_inc(ada_in[u], 16)
                for dst, src in ((cT, "cT"), (vec, "vec"), (bada, "bada"), (ident, "ident")):
                    sp.dma_start(dst[:], I[src]).then_inc(small_in, 16)
                sp.dma_start(xT[:, :, :], I["xT"].rearrange("(k p) t -> p k t", p=P)).then_inc(x_in, 16)
                ada_load(0, 0)
                ada_load(1, 1)
                sp.dma_start(brow[:, :], I["b_g2"].partition_broadcast(P)).then_inc(small_in, 16)
                with sp.Fori(1, 6) as i:
                    for u in range(2):
                        sp.wait_ge(ada_used, i * 2 + (u - 1))
                        ada_load(i * 2 + u, u)
                sp.wait_ge(ones_ready, 4)
                wab_load(sp, 0)
                for j in range(6):
                    w_in_load(sp, 0, j)
                sp.wait_ge(g2_ready, 4)
                sp.dma_start(S["g2"][0], g2b[:, 0, :]).then_inc(g2_out, 16)
                sp.dma_start(S["g2"][1, 0:TS], g2b[0:TS, 1, :]).then_inc(g2_out, 16)
                sp.wait_ge(g2_out, 32)

            @block.scalar
            def _(act):
                act.wait_ge(small_in, 80)
                act.activation(scT[:, :, :], cT[:, :, :], ACT.Silu).then_inc(sc_ready, 1)
                al_(act.activation(lam[0][:, :], vec[:, V_LAM, :], ACT.Abs))
                act.activation(lam[1][:, :], lam[0][:, :], ACT.Exp, scale=-1.0).then_inc(e_ready, 1)
                act.wait_ge(u_ready, 1)
                act.activation(lam[3][:, :], lam[2][:, :], ACT.Ln).then_inc(ln_ready, 1)
                act.wait_ge(x_in, 16)
                for k in range(KC):
                    if k >= 2:
                        act.wait_ge(sq_used, k - 1)
                    act.activation(sq[k % 2][:, :], xT[:, k, :], ACT.Square).then_inc(sq_ready, 1)
                act.wait_ge(ssum_ready, 1)
                act.wait_ge(ones_ready, 4)
                act.activation(rstd[:, :], pj[:, 0:T], ACT.Sqrt, bias=epsb[:, 0:1], scale=1.0 / D).then_inc(sd_ready, 1)

            @block.tensor
            def _(pe):
                pe.wait_ge(ones_ready, 4)
                for k in range(KC):
                    pe.wait_ge(sq_ready, k + 1)
                    for a, b in SLICES:
                        mm = pe.matmul(pj[:, a:b], ones[:, :], sq[k % 2][:, a:b], start=(k == 0), stop=(k == KC - 1))
                    mm.then_inc(sq_used, 1)
                mm2 = None
                pe.wait_ge(sq_used, KC)
                pe.sem_inc(ssum_ready, 1)
                pe.wait_ge(sc_ready, 1)

                def slab(i, u, first):
                    pe.wait_ge(ada_in[u], i * 16 + 16)
                    if not first:
                        pe.wait_ge(mod_read, i * 2 + (u - 1))
                    for m in range(ADA_CH):
                        for k in range(KC):
                            mm = pe.matmul(R[u][:, m * 9:m * 9 + 9], ada[u][:, k, m * P:(m + 1) * P], scT[:, k, :],
                                           start=(k == 0), stop=(k == KC - 1))
                    mm.then_inc(mod_ps, 1)
                    pe.wait_ge(mod_ps, i * 2 + (u + 1))
                    pe.sem_inc(ada_used, 1)
                slab(0, 0, True)
                slab(0, 1, True)
                with pe.Fori(1, 5) as i:
                    slab(i, 0, False)
                    slab(i, 1, False)
                pe.wait_ge(rep_ready, 2)
                pe.wait_ge(mod_read, 10)
                for u in range(2):
                    pe.wait_ge(ada_in[u], 96)
                    for k in range(KC):
                        pe.matmul(pk[:, u * 512:(u + 1) * 512], rep[:, k, 0:P], ada[u][:, k, :], start=(k == 0), stop=(k == KC - 1))
                    for k in range(KC):
                        mm = pe.matmul(R[u][0:TS, :], rep[:, k, P:P + TS], ada[u][:, k, :], start=(k == 0), stop=(k == KC - 1))
                    mm.then_inc(g2_ps, 1)

            @block.vector
            def _(v):
                v.memset(ones[:, :], 1.0).then_inc(ones_ready, 1)
                v.memset(onesm[:, :], 1.0 / P).then_inc(ones_ready, 1)
                v.memset(wab[:, :, :], 0.0).then_inc(ones_ready, 1)
                v.memset(epsb[:, :], EPS).then_inc(ones_ready, 1)
                v.memset(hnT[:, :, T:TPAD], 0.0)
                v.wait_ge(e_ready, 1)
                v.tensor_scalar(lam[2][:, :], lam[1][:, :], 1.0, None, ALU.add).then_inc(u_ready, 1)
                v.wait_ge(u_ready, 1)
                dl_(v.tensor_scalar(lam[4][:, :], lam[2][:, :], -1.0, None, ALU.add))
                dl_(v.tensor_tensor(lam[4][:, :], lam[1][:, :], lam[4][:, :], ALU.subtract))
                dl_(v.reciprocal(coef[:, :], lam[2][:, :]))
                dl_(v.tensor_tensor(lam[4][:, :], lam[4][:, :], coef[:, :], ALU.mult))
                v.wait_ge(ln_ready, 1)
                dl_(v.tensor_tensor(lam[4][:, :], lam[4][:, :], lam[3][:, :], ALU.add))
                dl_(v.tensor_scalar(coef[:, :], vec[:, V_LAM, :], -1.0, 0.0, ALU.mult, ALU.max))
                dl_(v.tensor_tensor(lam[4][:, :], lam[4][:, :], coef[:, :], ALU.add))
                dl_(v.tensor_scalar(coef[:, :], lam[4][:, :], -8.0, None, ALU.mult))
                v.wait_ge(sc_ready, 1)
                v.tensor_copy(rep[:, :, 0:P], scT[:, :, 0:1].broadcast_to([P, KC, P])).then_inc(rep_ready, 1)
                v.tensor_copy(rep[:, :, P:].rearrange("p k (b t) -> p k b t", t=NS), bc(scT[:, :, 1:1 + NB], 3, [P, KC, NB, NS])).then_inc(rep_ready, 1)
                v.wait_ge(sd_ready, 1)
                dl_(v.reciprocal(rstd[:, :], rstd[:, :]))

                def mod(i, u):
                    s = i * 2 + u
                    v.wait_ge(mod_ps, s + 1)
                    v.tensor_tensor(modT[:, bass.ds(s * ADA_CH, ADA_CH), :], R[u][:, 0:36].rearrange("p (m c) -> p m c", c=9),
                                    bc(bada[:, bass.ds(s * ADA_CH, ADA_CH)], 2, [P, ADA_CH, 9]), ALU.add).then_inc(mod_read, 1)
                with v.Fori(0, 5) as i:
                    mod(i, 0)
                    mod(i, 1)
                v.wait_ge(mod_read, 10)
                dl_(v.scalar_tensor_tensor(gain[:, :, :], modT[:, SC1:SC1 + 8, :], 1.0, bc(vec[:, V_N1, :], 2, [P, KC, 9]), ALU.add, ALU.mult))
                adjust(dl_, xT, hnT, rstd, gain, modT[:, SH1:SH1 + 8, :], tmp0)
                for u in range(2):
                    v.wait_ge(g2_ps, u + 1)
                    c = slice(u * 512, (u + 1) * 512)
                    v.tensor_tensor(g2b[:, 0, c], pk[:, c], brow[:, c], ALU.add).then_inc(g2_ready, 1)
                    v.tensor_tensor(g2b[0:TS, 1, c], R[u][0:TS, :], brow[0:TS, c], ALU.add).then_inc(g2_ready, 1)
        for ch in (dl_, al_, gl_):
            ch.flat()
        s0.close()

        s1 = ExitStack()
        rope_c, rope_s = sb(s1, "rope_c", [P, NT, DK]), sb(s1, "rope_s", [P, NT, DK])
        dmask, smask = sb(s1, "dmask", [P, H, P]), sb(s1, "smask", [TS, H, TS])
        xi, zeta, szeta = sb(s1, "xi", [DK, H, P]), sb(s1, "zeta", [P, H]), sb(s1, "szeta", [TS, H, NB])
        gch = sb(s1, "gch", [DK, 2, H])
        h0, c0 = sb(s1, "h0", [P, KC, NB]), sb(s1, "c0", [P, KC, NB * HIST])
        tok = sb(s1, "tok", [P, NT, CW])
        qkr = sb(s1, "qkr", [P, NT, 2, DK])
        rt = sb(s1, "rt", [P, NT, 2, DK])
        qT, kT, qxi = sb(s1, "qT", [DK, TPAD]), sb(s1, "kT", [DK, TPAD]), sb(s1, "qxi", [DK, T])
        pT, pTs = sb(s1, "pT", [P, NT - 1, P]), sb(s1, "pTs", [TS, TS])
        kz, kzb = sb(s1, "kz", [P, NT - 1, DK]), sb(s1, "kzb", [TS, NB, DK])
        Sall = sb(s1, "Sall", [DK, NT, P])
        S0, Sout = sb(s1, "S0", [DK, NB, P]), sb(s1, "Sout", [DK, NB, P])
        xr = sb(s1, "xr", [P, XR + NB * (HIST + NS)])
        xl, rg, ig, th, om = (sb(s1, n, [P, T]) for n in ("xl", "rg", "ig", "th", "om"))
        AS = SEQ + NB * (NS + 1)
        la, lb, lh = (sb(s1, n, [P, AS]) for n in ("la", "lb", "lh"))
        glru, gret, gate = (sb(s1, n, [P, T]) for n in ("glru", "gret", "gate"))
        osb, dsq = sb(s1, "osb", [P, T]), sb(s1, "dsq", [P, T])
        convo, lruo = sb(s1, "convo", [P, KC, (1 + NB) * HIST]), sb(s1, "lruo", [P, KC, 1 + NB])

        def seqs(ap, w):
            return ap.rearrange("p (b t) -> p b t", t=w)

        xrs = seqs(xr[:, XR:], HIST + NS)
        las, lbs, lhs_ = (seqs(t[:, SEQ:], NS + 1) for t in (la, lb, lh))

        tab_in, S0_in, S0_used = sem("tab_in"), sem("S0_in"), sem("S0_used")
        pj_ready, pk_ready, pj_free, pk_free = sem("pj_ready"), sem("pk_ready"), sem("pj_free"), sem("pk_free")
        w_used = [sem(f"w_used{j}") for j in range(6)]
        wab_used = sem("wab_used")
        st_ready, st_free, var_free = sem("st_ready"), sem("st_free"), sem("var_free")
        qkv_ready, xr_ready, xr_used = sem("qkv_ready"), sem("xr_ready"), sem("xr_used")
        rope_ready, glru_ready, gret_ready, ga_ready, ga_used, gb_ready = (sem(n) for n in ("rope_ready", "glru_ready", "gret_ready", "ga_ready", "ga_used", "gb_ready"))
        xl_ready, r_ready, i_ready, th_ready, a_ready, m2_ready, mult_ready = (sem(n) for n in ("xl_ready", "r_ready", "i_ready", "th_ready", "a_ready", "m2_ready", "mult_ready"))
        qkT_ready, pT_ready, kz_ready, S_ready, Sout_ready, o_ready, d_ready, dsq_ready, sdv_ready = (sem(n) for n in ("qkT_ready", "pT_ready", "kz_ready", "S_ready", "Sout_ready", "o_ready", "d_ready", "dsq_ready", "sdv_ready"))
        mg_ready, mg_out, st_out, lo_out, b_used, f_done = (sem(n) for n in ("mg_ready", "mg_out", "st_out", "lo_out", "b_used", "f_done"))
        NST, NVAR = 18, 3

        with nc.Block() as block:
            @block.sync
            def _(sp):
                for dst, src in ((rope_c, "rope_c"), (rope_s, "rope_s"), (dmask, "dmask"), (smask, "smask"), (xi, "xi"),
                                 (zeta, "zeta"), (szeta, "szeta"), (gch, "gch"), (h0, "h0"), (c0, "c0")):
                    sp.dma_start(dst[:], I[src]).then_inc(tab_in, 16)

                def s0_load(f):
                    src = I["state_ret"][:, bass.ds(f, 1)].rearrange("b o k v -> k (b o) v")
                    sp.dma_start(S0[:, :, :], src).then_inc(S0_in, 16)
                s0_load(0)

                def group(f, last):
                    if not last:
                        for j in range(6):
                            sp.wait_ge(w_used[j], f + 1)
                            w_in_load(sp, f + 1, j)
                        sp.wait_ge(wab_used, f + 1)
                        wab_load(sp, f + 1)
                    sp.wait_ge(S_ready, f + 1)
                    sp.dma_start(O["ret_prompt"][bass.ds(f, 1)].rearrange("o k v -> k (o v)"), Sall[:, NT - 1, :]).then_inc(st_out, 16)
                    sp.wait_ge(Sout_ready, f * 2 + 2)
                    sp.dma_start(O["ret_sample"][:, bass.ds(f, 1)].rearrange("b o k v -> k (b o) v"), Sout[:, :, :]).then_inc(st_out, 16)
                    if not last:
                        sp.wait_ge(S0_used, f + 1)
                        s0_load(f + 1)
                    sp.wait_ge(mg_ready, f + 1)
                    sp.dma_start(S["mg"][bass.ds(f, 1)].rearrange("o p t -> p (o t)"), osb[:, :]).then_inc(mg_out, 16)
                with sp.Fori(0, H - 1) as f:
                    group(f, False)
                group(H - 1, True)
                sp.dma_start(O["conv"], convo[:, :, :]).then_inc(lo_out, 16)
                sp.dma_start(O["lru"], lruo[:, :, :]).then_inc(lo_out, 16)
                sp.wait_ge(lo_out, 32)
                sp.wait_ge(st_out, 32 * H + 32)
                sp.wait_ge(mg_out, 16 * H + 16)

            @block.scalar
            def _(act):
                act.sem_inc(pj_free, 1)
                act.sem_inc(pk_free, 1)
                act.sem_inc(var_free, 1)
                act.wait_ge(tab_in, 160)
                with act.Fori(0, H) as f:
                    fs = bass.ds(f, 1)
                    act.wait_ge(pj_ready, f * 5 + 1)
                    act.activation(tok[:, 0:6, :], pj[:, :].rearrange("p (t c) -> p t c", c=CW), ACT.Copy).then_inc(pj_free, 1)
                    act.wait_ge(pk_ready, f * 4 + 1)
                    act.activation(tok[:, 6:9, :], pk[:, 0:3 * CW].rearrange("p (t c) -> p t c", c=CW), ACT.Copy).then_inc(qkv_ready, 1)
                    act.wait_ge(qkv_ready, f + 1)
                    act.sem_inc(pk_free, 1)
                    act.wait_ge(pj_ready, f * 5 + 2)
                    act.wait_ge(xr_used, f + 1)
                    act.activation(xr[:, HIST:XR], pj[:, 0:SEQ], ACT.Copy)
                    act.activation(xrs[:, :, 0:HIST], c0[:, fs, :].rearrange("p o (b j) -> p (o b) j", j=HIST), ACT.Copy)
                    act.activation(xrs[:, :, HIST:], seqs(pj[:, SEQ:T], NS), ACT.Copy).then_inc(xr_ready, 1)
                    act.wait_ge(xr_ready, f + 1)
                    act.sem_inc(pj_free, 1)
                    act.wait_ge(pk_ready, f * 4 + 2)
                    act.wait_ge(f_done, f + 1)
                    act.activation(glru[:, :], pk[:, 0:T], ACT.Gelu_apprx_tanh).then_inc(glru_ready, 1)
                    act.wait_ge(glru_ready, f + 1)
                    act.sem_inc(pk_free, 1)
                    act.wait_ge(pj_ready, f * 5 + 3)
                    act.activation(gret[:, :], pj[:, 0:T], ACT.Silu).then_inc(gret_ready, 1)
                    act.wait_ge(gret_ready, f + 1)
                    act.sem_inc(pj_free, 1)
                    act.wait_ge(pk_ready, f * 4 + 3)
                    act.activation(gate[:, :], pk[:, 0:T], ACT.Sigmoid).then_inc(ga_ready, 1)
                    act.wait_ge(ga_ready, f + 1)
                    act.sem_inc(pk_free, 1)
                    act.wait_ge(pj_ready, f * 5 + 4)
                    act.activation(rg[:, :], pj[:, 0:T], ACT.Sigmoid, bias=vec[:, V_BA, fs]).then_inc(r_ready, 1)
                    act.wait_ge(r_ready, f + 1)
                    act.sem_inc(pj_free, 1)
                    act.wait_ge(pk_ready, f * 4 + 4)
                    act.wait_ge(ga_used, f + 1)
                    act.activation(gate[:, :], pk[:, 0:T], ACT.Sigmoid).then_inc(gb_ready, 1)
                    act.wait_ge(gb_ready, f + 1)
                    act.sem_inc(pk_free, 1)
                    act.wait_ge(pj_ready, f * 5 + 5)
                    act.activation(ig[:, :], pj[:, 0:T], ACT.Sigmoid, bias=vec[:, V_BX, fs]).then_inc(i_ready, 1)
                    act.wait_ge(i_ready, f + 1)
                    act.sem_inc(pj_free, 1)
                    act.activation(th[:, :], rg[:, :], ACT.Tanh, scale=coef[:, fs]).then_inc(th_ready, 1)
                    act.activation(la[:, 0:SEQ], rg[:, 0:SEQ], ACT.Exp, scale=coef[:, fs])
                    act.activation(las[:, :, 1:], seqs(rg[:, SEQ:T], NS), ACT.Exp, scale=coef[:, fs]).then_inc(a_ready, 1)
                    act.wait_ge(m2_ready, f + 1)
                    act.activation(om[:, :], om[:, :], ACT.Sqrt).then_inc(mult_ready, 1)
                    act.wait_ge(d_ready, f + 1)
                    act.activation(dsq[:, :], osb[:, :], ACT.Square).then_inc(dsq_ready, 1)
                    for n, (a, b) in enumerate(SLICES):
                        act.wait_ge(st_ready, f * (NST + NVAR) + NST + 1 + n)
                        act.activation(dsq[:, a:b], R[n % 2][:, 0:b - a], ACT.Sqrt, bias=epsb[:, 0:1]).then_inc(sdv_ready, 1)
                    act.wait_ge(sdv_ready, f * 3 + 3)
                    act.sem_inc(var_free, 1)

            @block.tensor
            def _(pe):
                pe.wait_ge(tab_in, 160)
                with pe.Fori(0, H) as f:
                    use = {"pj": 0, "pk": 0}

                    def bank_wait(b):
                        pe.wait_ge(pj_free if b == "pj" else pk_free, f * (5 if b == "pj" else 4) + use[b] + 1)
                        use[b] += 1
                    pe.wait_ge(w_in_sems[0], f * 16 + 16)
                    bank_wait("pj")
                    bank_wait("pk")
                    for t in range(NT):
                        dst = pj[:, t * CW:(t + 1) * CW] if t < 6 else pk[:, (t - 6) * CW:(t - 5) * CW]
                        for k in range(KC):
                            mm = pe.matmul(dst, hnT[:, k, t * P:(t + 1) * P], w_qkv[:, k, :], start=(k == 0), stop=(k == KC - 1))
                        if t == 5:
                            mm.then_inc(pj_ready, 1)
                    mm.then_inc(pk_ready, 1)
                    pe.wait_ge(pk_ready, f * 4 + 1)
                    pe.sem_inc(w_used[0], 1)

                    def part(j, b, s, ready, count):
                        if s == 0:
                            pe.wait_ge(w_in_sems[j], f * 16 + 16)
                            bank_wait(b)
                        a, e = SLICES[s]
                        for k in range(KC):
                            mm = pe.matmul((pj if b == "pj" else pk)[:, a:e], w_part[j - 1][:, k, :], hnT[:, k, a:e], start=(k == 0), stop=(k == KC - 1))
                        if s == 2:
                            mm.then_inc(ready, 1)
                            pe.wait_ge(ready, count)
                            pe.sem_inc(w_used[j], 1)

                    def lru_gate(g, b, ready):
                        bank_wait(b)
                        for a, e in SLICES:
                            mm = pe.matmul((pj if b == "pj" else pk)[:, a:e], wab[:, g, :], xl[:, a:e], start=True, stop=True)
                        mm.then_inc(ready, 1)

                    st = [0]

                    def stage_wait():
                        n = st[0]
                        if n < 2:
                            pe.wait_ge(var_free, f + 1)
                        elif n <= NST + 1:
                            pe.wait_ge(st_free, f * NST + (n - 1))
                        else:
                            pe.wait_ge(sdv_ready, f * 3 + 1)
                        st[0] += 1
                        return R[n % 2]

                    def transposes(which, tiles):
                        r = stage_wait()
                        if which == 0 and tiles[0] == 0:
                            pe.wait_ge(rope_ready, f + 1)
                        hold(pe)
                        for n, (w, t) in enumerate([(which, t) for t in tiles] if tiles[0] < 8 else [(0, 8), (1, 8)]):
                            mm = pe.transpose(r[0:DK, n * P:(n + 1) * P], qkr[:, t, w, :], ident[:, :])
                        mm.then_inc(st_ready, 1)

                    def kv(c0_):
                        r = stage_wait()
                        pe.wait_ge(kz_ready, f + 1)
                        for n in range(4):
                            mm = pe.matmul(r[0:DK, n * P:(n + 1) * P], kz[:, c0_ + n, :], tok[:, c0_ + n, P:2 * P], start=True, stop=True)
                        mm.then_inc(st_ready, 1)

                    def score(c0_):
                        r = stage_wait()
                        pe.wait_ge(qkT_ready, f + 1)
                        for n in range(4):
                            c = slice((c0_ + n) * P, (c0_ + n + 1) * P)
                            mm = pe.matmul(r[:, n * P:(n + 1) * P], kT[:, c], qT[:, c], start=True, stop=True)
                        mm.then_inc(st_ready, 1)

                    def score_s():
                        r = stage_wait()
                        pe.wait_ge(qkT_ready, f + 1)
                        hold(pe)
                        mm = pe.matmul(r[0:TS, 0:TS], kT[:, SEQ:T], qT[:, SEQ:T], start=True, stop=True)
                        mm.then_inc(st_ready, 1)

                    def kv_s(b0):
                        r = stage_wait()
                        pe.wait_ge(kz_ready, f + 1)
                        hold(pe)
                        for n in range(4):
                            mm = pe.matmul(r[0:DK, n * P:(n + 1) * P], kzb[:, b0 + n, :], tok[0:TS, NT - 1, P:2 * P], start=True, stop=True)
                        mm.then_inc(st_ready, 1)

                    def outp(c0_):
                        r = stage_wait()
                        if c0_ == 0:
                            pe.wait_ge(pT_ready, f + 1)
                        for n in range(4):
                            c = c0_ + n
                            mm = pe.matmul(r[:, n * P:(n + 1) * P], tok[:, c, P:2 * P], pT[:, c, :], start=True, stop=(c == 0))
                            if c:
                                mm = pe.matmul(r[:, n * P:(n + 1) * P], Sall[:, c, :], qxi[:, c * P:(c + 1) * P], start=False, stop=True)
                        mm.then_inc(st_ready, 1)

                    def outp_s():
                        r = stage_wait()
                        pe.wait_ge(S0_in, f * 16 + 16)
                        pe.matmul(r[:, 0:TS], tok[0:TS, NT - 1, P:2 * P], pTs[:, :], start=True, stop=False)
                        for b in range(NB):
                            mm = pe.matmul(r[:, b * NS:(b + 1) * NS], S0[:, b, :], qxi[:, SEQ + b * NS:SEQ + (b + 1) * NS], start=False, stop=(b == NB - 1))
                        mm.then_inc(st_ready, 1)

                    def spread(s, src, wait):
                        a, e = SLICES[s]
                        r = stage_wait()
                        pe.wait_ge(*wait)
                        dst = r[:, 0:e - a]
                        mm = pe.matmul(dst, onesm[:, :], src[:, a:e], start=True, stop=True)
                        mm.then_inc(st_ready, 1)

                    for s in range(3):
                        part(1, "pj", s, pj_ready, f * 5 + 2)
                    part(2, "pk", 0, pk_ready, f * 4 + 2)
                    transposes(0, range(0, 4))
                    transposes(0, range(4, 8))
                    part(2, "pk", 1, pk_ready, f * 4 + 2)
                    part(2, "pk", 2, pk_ready, f * 4 + 2)
                    transposes(1, range(0, 4))
                    transposes(1, range(4, 8))
                    part(3, "pj", 0, pj_ready, f * 5 + 3)
                    transposes(0, (8,))
                    kv(0)
                    part(3, "pj", 1, pj_ready, f * 5 + 3)
                    part(3, "pj", 2, pj_ready, f * 5 + 3)
                    kv(4)
                    score(0)
                    part(4, "pk", 0, pk_ready, f * 4 + 3)
                    score(4)
                    score_s()
                    part(4, "pk", 1, pk_ready, f * 4 + 3)
                    part(4, "pk", 2, pk_ready, f * 4 + 3)
                    kv_s(0)
                    kv_s(4)
                    pe.wait_ge(xl_ready, f + 1)
                    pe.wait_ge(wab_in, f * 32 + 32)
                    lru_gate(0, "pj", pj_ready)
                    part(5, "pk", 0, pk_ready, f * 4 + 4)
                    outp(0)
                    outp(4)
                    part(5, "pk", 1, pk_ready, f * 4 + 4)
                    part(5, "pk", 2, pk_ready, f * 4 + 4)
                    outp_s()
                    lru_gate(1, "pj", pj_ready)
                    pe.wait_ge(pj_ready, f * 5 + 5)
                    pe.sem_inc(wab_used, 1)
                    for s in range(3):
                        spread(s, osb, (o_ready, f + 1))
                    for s in range(3):
                        spread(s, dsq, (dsq_ready, f + 1))
                    assert st[0] == NST + NVAR

            @block.vector
            def _(v):
                v.sem_inc(xr_used, 1)
                v.sem_inc(f_done, 1)
                v.sem_inc(st_out, 32)
                v.sem_inc(mg_out, 16)
                v.memset(xr[:, 0:HIST], 0.0)
                v.memset(las[:, :, 0:1], 0.0)
                v.wait_ge(tab_in, 160)
                with v.Fori(0, H) as f:
                    fs = bass.ds(f, 1)
                    dl_.loop(f, 23)
                    st = [0]

                    def stage():
                        st[0] += 1
                        v.wait_ge(st_ready, f * (NST + NVAR) + st[0])
                        return R[(st[0] - 1) % 2]
                    v.wait_ge(qkv_ready, f + 1)
                    qk = tok[:, :, 0:2 * DK].rearrange("p t (w d) -> p t w d", w=2)
                    sh = [P, NT, 2, DK]
                    v.tensor_tensor(qkr[:, :, :, :], qk, bc(rope_c[:, :, :], 2, sh), ALU.mult)
                    hf = DK // 2
                    sh = [P, NT, 2, hf]
                    v.tensor_tensor(rt[:, :, :, 0:hf], qk[:, :, :, hf:], bc(rope_s[:, :, 0:hf], 2, sh), ALU.mult)
                    dl_(v.tensor_tensor(rt[:, :, :, hf:], qk[:, :, :, 0:hf], bc(rope_s[:, :, hf:], 2, sh), ALU.mult))
                    v.tensor_tensor(qkr[:, :, :, :], qkr[:, :, :, :], rt[:, :, :, :], ALU.add).then_inc(rope_ready, 1)
                    v.wait_ge(rope_ready, f + 1)
                    v.tensor_scalar(kz[:, :, :], qkr[:, 0:NT - 1, 1, :], zeta[:, fs], None, ALU.mult)
                    v.tensor_tensor(kzb[:, :, :], bc(qkr[0:TS, NT - 1, 1, :], 1, [TS, NB, DK]),
                                    szeta[:, fs, :].rearrange("p o b -> p (o b)").unsqueeze(2).broadcast_to([TS, NB, DK]), ALU.mult).then_inc(kz_ready, 1)
                    v.wait_ge(xr_ready, f + 1)
                    xls = seqs(xl[:, SEQ:T], NS)
                    v.tensor_scalar(xl[:, 0:SEQ], xr[:, 0:SEQ], vec[:, V_CW, fs], vec[:, V_CB, fs], ALU.mult, ALU.add)
                    dl_(v.tensor_scalar(xls, xrs[:, :, 0:NS], vec[:, V_CW, fs], vec[:, V_CB, fs], ALU.mult, ALU.add))
                    for j in range(1, CONV):
                        v.scalar_tensor_tensor(xl[:, 0:SEQ], xr[:, j:j + SEQ], vec[:, V_CW + j, fs], xl[:, 0:SEQ], ALU.mult, ALU.add)
                        ins = v.scalar_tensor_tensor(xls, xrs[:, :, j:j + NS], vec[:, V_CW + j, fs], xls, ALU.mult, ALU.add)
                        if j < CONV - 1:
                            dl_(ins)
                        else:
                            ins.then_inc(xl_ready, 1)
                    v.tensor_copy(convo[:, fs, 0:HIST], xr[:, SEQ:XR].unsqueeze(1))
                    v.tensor_copy(convo[:, fs, HIST:].rearrange("p o (b j) -> p (o b) j", j=HIST), xrs[:, :, NS:]).then_inc(xr_used, 1)
                    for n in range(2):
                        r = stage()
                        v.tensor_copy(qT[:, n * 512:(n + 1) * 512], r[0:DK, :]).then_inc(st_free, 1)
                    for n in range(2):
                        r = stage()
                        v.tensor_scalar(kT[:, n * 512:(n + 1) * 512], r[0:DK, :], DK ** -0.5, None, ALU.mult).then_inc(st_free, 1)
                    r = stage()
                    dl_(v.tensor_copy(qT[:, SEQ:TPAD], r[0:DK, 0:P]))
                    v.tensor_scalar(kT[:, SEQ:TPAD], r[0:DK, P:2 * P], DK ** -0.5, None, ALU.mult).then_inc(qkT_ready, 1)
                    v.wait_ge(qkT_ready, f + 1)
                    v.sem_inc(st_free, 1)
                    v.tensor_tensor(seqs(qxi[:, 0:SEQ], P), seqs(qT[:, 0:SEQ], P), xi[:, fs, :].broadcast_to([DK, NT - 1, P]), ALU.mult)
                    dl_(v.tensor_tensor(seqs(qxi[:, SEQ:T], NS), seqs(qT[:, SEQ:T], NS), xi[:, fs, 0:NS].broadcast_to([DK, NB, NS]), ALU.mult))
                    v.wait_ge(st_out, f * 32 + 32)
                    for q in range(2):
                        r = stage()
                        for n in range(4):
                            c = 4 * q + n
                            kvp = r[0:DK, n * P:(n + 1) * P]
                            if c == 0:
                                ins = v.tensor_copy(Sall[:, 1, :], kvp)
                            else:
                                ins = v.scalar_tensor_tensor(Sall[:, c + 1, :], Sall[:, c, :], gch[:, 0, fs], kvp, ALU.mult, ALU.add)
                            if c < 7:
                                dl_(ins)
                            else:
                                ins.then_inc(S_ready, 1)
                                v.wait_ge(S_ready, f + 1)
                        v.sem_inc(st_free, 1)
                    for q in range(2):
                        r = stage()
                        v.tensor_tensor(pT[:, 4 * q:4 * q + 4, :], seqs(r[:, :], P), dmask[:, fs, :].broadcast_to([P, 4, P]), ALU.mult).then_inc(st_free, 1)
                    r = stage()
                    v.tensor_tensor(pTs[:, :], r[0:TS, 0:TS], smask[:, fs, :].rearrange("p o m -> p (o m)"), ALU.mult).then_inc(pT_ready, 1)
                    v.wait_ge(pT_ready, f + 1)
                    v.sem_inc(st_free, 1)
                    v.wait_ge(S0_in, f * 16 + 16)
                    for q in range(2):
                        r = stage()
                        v.scalar_tensor_tensor(Sout[:, 4 * q:4 * q + 4, :], S0[:, 4 * q:4 * q + 4, :], gch[:, 1, fs], seqs(r[0:DK, :], P), ALU.mult, ALU.add).then_inc(Sout_ready, 1)
                        v.wait_ge(Sout_ready, f * 2 + q + 1)
                        v.sem_inc(st_free, 1)
                    v.wait_ge(gret_ready, f + 1)
                    v.wait_ge(ga_ready, f + 1)
                    v.tensor_tensor(gret[:, :], gret[:, :], gate[:, :], ALU.mult).then_inc(ga_used, 1)
                    v.wait_ge(mg_out, f * 16 + 16)
                    for q in range(2):
                        r = stage()
                        v.tensor_copy(osb[:, q * 512:(q + 1) * 512], r[:, :]).then_inc(st_free, 1)
                    r = stage()
                    v.tensor_copy(osb[:, SEQ:T], r[:, 0:TS]).then_inc(o_ready, 1)
                    v.wait_ge(o_ready, f + 1)
                    v.sem_inc(st_free, 1)
                    v.sem_inc(S0_used, 1)
                    v.wait_ge(th_ready, f + 1)
                    dl_(v.tensor_scalar(om[:, :], th[:, :], -1.0, 1.0, ALU.mult, ALU.add))
                    dl_(v.reciprocal(om[:, :], om[:, :]))
                    v.scalar_tensor_tensor(om[:, :], th[:, :], -2.0, om[:, :], ALU.mult, ALU.mult).then_inc(m2_ready, 1)
                    v.wait_ge(i_ready, f + 1)
                    dl_(v.tensor_tensor(ig[:, :], ig[:, :], xl[:, :], ALU.mult))
                    for n, (a, b) in enumerate(SLICES):
                        r = stage()
                        src = r[:, 0:b - a]
                        ins = v.tensor_tensor(osb[:, a:b], osb[:, a:b], src, ALU.subtract)
                        ins.then_inc(st_free if n < 2 else d_ready, 1)
                    v.wait_ge(d_ready, f + 1)
                    v.sem_inc(st_free, 1)
                    assert st[0] == NST
                    v.wait_ge(mult_ready, f + 1)
                    v.wait_ge(a_ready, f + 1)
                    v.tensor_copy(lbs[:, :, 0:1], h0[:, fs, :].rearrange("p o b -> p (o b)").unsqueeze(2))
                    v.tensor_tensor(lb[:, 0:SEQ], ig[:, 0:SEQ], om[:, 0:SEQ], ALU.mult)
                    dl_(v.tensor_tensor(lbs[:, :, 1:], seqs(ig[:, SEQ:T], NS), seqs(om[:, SEQ:T], NS), ALU.mult))
                    dl_(v.tensor_tensor_scan(lh[:, :], la[:, :], lb[:, :], 0.0, ALU.mult, ALU.add))
                    v.tensor_copy(lruo[:, fs, 0:1], lh[:, SEQ - 1:SEQ].unsqueeze(1))
                    v.tensor_copy(lruo[:, fs, 1:], lhs_[:, :, NS].unsqueeze(1))
                    v.wait_ge(glru_ready, f + 1)
                    v.tensor_tensor(glru[:, 0:SEQ], glru[:, 0:SEQ], lh[:, 0:SEQ], ALU.mult)
                    dl_(v.tensor_tensor(seqs(glru[:, SEQ:T], NS), seqs(glru[:, SEQ:T], NS), lhs_[:, :, 1:], ALU.mult))
                    v.wait_ge(gb_ready, f + 1)
                    dl_(v.tensor_tensor(glru[:, :], glru[:, :], gate[:, :], ALU.mult))
                    v.wait_ge(sdv_ready, f * 3 + 3)
                    dl_(v.reciprocal(dsq[:, :], dsq[:, :]))
                    dl_(v.scalar_tensor_tensor(osb[:, :], osb[:, :], vec[:, V_GN, fs], dsq[:, :], ALU.mult, ALU.mult))
                    dl_(v.tensor_tensor(osb[:, :], osb[:, :], gret[:, :], ALU.mult))
                    v.tensor_tensor(osb[:, :], osb[:, :], glru[:, :], ALU.add).then_inc(mg_ready, 1)
                    v.wait_ge(mg_ready, f + 1)
                    v.sem_inc(f_done, 1)
                dl_.end(H)
        for ch in (al_, gl_):
            ch.flat()
        s1.close()
        mix.close()

        late = ExitStack()
        hn2T = sb(late, "hn2T", [P, KC, T])
        s2 = ExitStack()
        mgT, x2T = sb(s2, "mgT", [P, KC, T]), sb(s2, "x2T", [P, KC, T])
        wo = sb(s2, "wo", [P, KC, D])
        sq2 = [sb(s2, f"sqb{u}", [P, T]) for u in range(2)]
        rstd2, gain2, tmp2 = sb(s2, "rstd2", [P, T]), sb(s2, "gain2", [P, KC, 1 + NB]), sb(s2, "tmp2", [P, KC, TS])
        stg = [sb(s2, f"stg{u}", [P, D]) for u in range(2)]
        mgi, wo_in, x2_in = sem("mgi"), sem("wo_in"), sem("x2_in")
        o2_ready, o2_free, x2_ready, sq2_ready, ssum2, sd2 = (sem(n) for n in ("o2_ready", "o2_free", "x2_ready", "sq2_ready", "ssum2", "sd2"))
        hn2_ready, tr_ready, tr_free, stg_ready = (sem(n) for n in ("hn2_ready", "tr_ready", "tr_free", "stg_ready"))
        stg_out = [sem("stg_out0"), sem("stg_out1")]

        with nc.Block() as block:
            @block.sync
            def _(sp):
                for k in range(KC):
                    sp.dma_start(wo[:, k, :], I["w_out"][k * P:(k + 1) * P, :]).then_inc(wo_in, 16)
                sp.dma_start(mgT[:, :, :], S["mg"].rearrange("f p t -> p f t")).then_inc(mgi, 16)
                sp.dma_start(x2T[:, :, :], I["xT"].rearrange("(k p) t -> p k t", p=P)).then_inc(x2_in, 16)
                for n in range(2 * NT):
                    sp.wait_ge(stg_ready, n + 1)
                    rows = P if n // 2 < NT - 1 else TS
                    sp.dma_start(S["x2" if n % 2 == 0 else "hn2"][n // 2, 0:rows], stg[n % 2][0:rows, :]).then_inc(stg_out[n % 2], 16)
                for u in range(2):
                    sp.wait_ge(stg_out[u], 16 * NT)

            @block.tensor
            def _(pe):
                pe.wait_ge(wo_in, 16 * KC)
                pe.wait_ge(mgi, 16)
                for m in range(KC):
                    acc = pj if m % 2 == 0 else pk
                    if m >= 2:
                        pe.wait_ge(o2_free, m - 1)
                    for a, e in SLICES:
                        for k in range(KC):
                            mm = pe.matmul(acc[:, a:e], wo[:, k, m * P:(m + 1) * P], mgT[:, k, a:e], start=(k == 0), stop=(k == KC - 1))
                    mm.then_inc(o2_ready, 1)
                pe.wait_ge(o2_free, KC)
                for k in range(KC):
                    pe.wait_ge(sq2_ready, k + 1)
                    for a, e in SLICES:
                        mm = pe.matmul(pj[:, a:e], ones[:, :], sq2[k % 2][:, a:e], start=(k == 0), stop=(k == KC - 1))
                    mm.then_inc(ssum2, 1)
                pe.wait_ge(hn2_ready, 1)
                n = 0
                for t in range(NT):
                    c = slice(t * P, min((t + 1) * P, T))
                    w = c.stop - c.start
                    for src in (x2T, hn2T):
                        for q in range(2):
                            if n >= 2:
                                pe.wait_ge(tr_free, n - 1)
                            for j in range(4):
                                mm = pe.transpose(R[n % 2][0:w, j * P:(j + 1) * P], src[:, 4 * q + j, c], ident[:, :])
                            mm.then_inc(tr_ready, 1)
                            n += 1

            @block.scalar
            def _(act):
                for k in range(KC):
                    act.wait_ge(x2_ready, k + 1)
                    if k >= 2:
                        act.wait_ge(ssum2, k - 1)
                    act.activation(sq2[k % 2][:, :], x2T[:, k, :], ACT.Square).then_inc(sq2_ready, 1)
                act.wait_ge(ssum2, KC)
                act.activation(rstd2[:, :], pj[:, 0:T], ACT.Sqrt, bias=epsb[:, 0:1], scale=1.0 / D).then_inc(sd2, 1)
                n = 0
                for t in range(NT):
                    w = P if t < NT - 1 else TS
                    for s in range(2):
                        if t >= 1:
                            act.wait_ge(stg_out[s], 16 * t)
                        for q in range(2):
                            act.wait_ge(tr_ready, n + 1)
                            act.activation(stg[s][0:w, q * 512:(q + 1) * 512], R[n % 2][0:w, :], ACT.Copy).then_inc(tr_free, 1)
                            n += 1
                        act.wait_ge(tr_free, n)
                        act.sem_inc(stg_ready, 1)

            @block.vector
            def _(v):
                v.wait_ge(x2_in, 16)
                for m in range(KC):
                    acc = pj if m % 2 == 0 else pk
                    v.wait_ge(o2_ready, m + 1)
                    v.scalar_tensor_tensor(x2T[:, m, 0:SEQ], acc[:, 0:SEQ], modT[:, G1 + m, 0:1], x2T[:, m, 0:SEQ], ALU.mult, ALU.add)
                    dl_(v.tensor_tensor(seqs(tmp2[:, m, :], NS), seqs(acc[:, SEQ:T], NS), bc(modT[:, G1 + m, 1:1 + NB], 2, [P, NB, NS]), ALU.mult))
                    v.tensor_tensor(x2T[:, m, SEQ:T], x2T[:, m, SEQ:T], tmp2[:, m, :], ALU.add).then_inc(x2_ready, 1)
                    v.sem_inc(o2_free, 1)
                dl_(v.scalar_tensor_tensor(gain2[:, :, :], modT[:, SC2:SC2 + 8, :], 1.0, bc(vec[:, V_N2, :], 2, [P, KC, 9]), ALU.add, ALU.mult))
                v.wait_ge(sd2, 1)
                dl_(v.reciprocal(rstd2[:, :], rstd2[:, :]))
                adjust(dl_, x2T, hn2T, rstd2, gain2, modT[:, SH2:SH2 + 8, :], tmp2)
                v.sem_inc(hn2_ready, 1)
        dl_.flat()
        s2.close()

        s3 = ExitStack()
        wq = [sb(s3, f"wq{u}", [P, KC, P]) for u in range(2)]
        keys = sb(s3, "keys", [P, 2, NKEY])
        qh = [sb(s3, f"qh{u}", [P, T]) for u in range(2)]
        sc = [sb(s3, f"sc{u}", [P, NT, NKEY]) for u in range(2)]
        tv = [sb(s3, f"tv{u}", [P, NT, TOPK]) for u in range(2)]
        ti = [sb(s3, f"ti{u}", [P, NT, TOPK], U32) for u in range(2)]
        tf = [sb(s3, f"tf{u}", [P, NT, TOPK]) for u in range(2)]
        cand, cid = sb(s3, "cand", [P, NT, NCAND]), sb(s3, "cid", [P, NT, NCAND])
        bv = sb(s3, "bv", [P, NT, TOPK])
        bp, bpf = sb(s3, "bp", [P, NT, TOPK], U32), sb(s3, "bpf", [P, NT, TOPK])
        hot = sb(s3, "hot", [P, NT, TOPK, NCAND])
        iota = sb(s3, "iota", [P, NCAND])
        eidf = sb(s3, "eidf", [P, NT, H, TOPK])
        gsum = sb(s3, "gsum", [P, NT * H])
        wq_in, wq_used = [sem("wq_in0"), sem("wq_in1")], sem("wq_used")
        key_in, q_ps, qh_ready, s_ps, s_ready, s_used, z_ready = (sem(n) for n in ("key_in", "q_ps", "qh_ready", "s_ps", "s_ready", "s_used", "z_ready"))
        pos_ready, hot_ready, hot_used, exp_ready, max_ready = (sem(n) for n in ("pos_ready", "hot_ready", "hot_used", "exp_ready", "max_ready"))

        with nc.Block() as block:
            @block.sync
            def _(sp):
                sp.dma_start(keys[:, :, :], I["keys"]).then_inc(key_in, 16)
                sp.dma_start(iota[:, :], I["iota"]).then_inc(key_in, 16)

                def load(h, u):
                    src = I["peer_wq"][:, bass.ds(h * 256 + u * P, P)].rearrange("(k p) n -> p k n", p=P)
                    sp.dma_start(wq[u][:, :, :], src).then_inc(wq_in[u], 16)
                load(0, 0)
                load(0, 1)
                with sp.Fori(1, H) as h:
                    for u in range(2):
                        sp.wait_ge(wq_used, h * 2 + (u - 1))
                        load(h, u)

            @block.tensor
            def _(pe):
                pe.wait_ge(key_in, 32)
                with pe.Fori(0, H) as h:
                    for u in range(2):
                        acc = (pj, pk)[u]
                        pe.wait_ge(wq_in[u], h * 16 + 16)
                        pe.wait_ge(s_ready, h * 2 + (u + 1))
                        for a, e in SLICES:
                            for k in range(KC):
                                mm = pe.matmul(acc[:, a:e], wq[u][:, k, :], hn2T[:, k, a:e], start=(k == 0), stop=(k == KC - 1))
                        mm.then_inc(q_ps, 1)
                        pe.wait_ge(q_ps, h * 2 + (u + 1))
                        pe.sem_inc(wq_used, 1)
                    for u in range(2):
                        acc = (pj, pk)[u]
                        pe.wait_ge(qh_ready, h * 2 + (u + 1))
                        for t in range(NT):
                            c = slice(t * P, min((t + 1) * P, T))
                            mm = pe.matmul(acc[0:c.stop - c.start, t * NKEY:(t + 1) * NKEY], qh[u][:, c], keys[:, u, :], start=True, stop=True)
                        mm.then_inc(s_ps, 1)

            @block.scalar
            def _(act):
                act.sem_inc(s_ready, 2)
                act.wait_ge(z_ready, 2)
                with act.Fori(0, H) as h:
                    for u in range(2):
                        act.wait_ge(q_ps, h * 2 + (u + 1))
                        act.activation(qh[u][:, :], (pj, pk)[u][:, 0:T], ACT.Copy).then_inc(qh_ready, 1)
                    for u in range(2):
                        acc = (pj, pk)[u]
                        act.wait_ge(s_ps, h * 2 + (u + 1))
                        act.wait_ge(s_used, h * 2 + (u + 1))
                        act.activation(sc[u][:, 0:8, :], acc[:, 0:SEQ].rearrange("p (t n) -> p t n", n=NKEY), ACT.Copy)
                        act.activation(sc[u][0:TS, 8, :], acc[0:TS, SEQ:SEQ + NKEY], ACT.Copy).then_inc(s_ready, 1)
                act.wait_ge(max_ready, 1)
                act.activation(gw[:, :, :, :], gw[:, :, :, :], ACT.Exp).then_inc(exp_ready, 1)

            @block.gpsimd
            def _(g):
                g.wait_ge(key_in, 32)
                with g.Fori(0, H) as h:
                    g.wait_ge(pos_ready, h + 1)
                    ins = g.tensor_tensor(hot[:, :, :, :], hot[:, :, :, :], bc(cid[:, :, :], 2, [P, NT, TOPK, NCAND]), ALU.mult)
                    ins.then_inc(hot_ready, 1)

            @block.vector
            def _(v):
                v.sem_inc(s_used, 2)
                v.sem_inc(hot_used, 1)
                for u in range(2):
                    v.memset(sc[u][64:128, 8, :], 0.0).then_inc(z_ready, 1)
                v.wait_ge(key_in, 32)

                def top16(src, vals, idxs):
                    hold(v)
                    for t in range(NT):
                        ins = v.max(vals[:, t, 0:8], src[:, t, :])
                    dl_(ins)
                    hold(v)
                    for t in range(NT):
                        v.max_index(idxs[:, t, 0:8], vals[:, t, 0:8], src[:, t, :])
                    for t in range(NT):
                        ins = v.match_replace(src[:, t, :], vals[:, t, 0:8], src[:, t, :], LOW)
                    dl_(ins)
                    hold(v)
                    for t in range(NT):
                        ins = v.max(vals[:, t, 8:16], src[:, t, :])
                    dl_(ins)
                    hold(v)
                    for t in range(NT):
                        ins = v.max_index(idxs[:, t, 8:16], vals[:, t, 8:16], src[:, t, :])
                    dl_(ins)

                with v.Fori(0, H) as h:
                    hs = bass.ds(h, 1)
                    dl_.loop(h, 17)
                    for u in range(2):
                        v.wait_ge(s_ready, h * 2 + (u + 3))
                        top16(sc[u], tv[u], ti[u])
                        v.sem_inc(s_used, 1)
                        dl_(v.tensor_scalar(tf[u][:, :, :], ti[u][:, :, :], float(NKEY) if u == 0 else 1.0, None, ALU.mult))
                    v.wait_ge(hot_used, h + 1)
                    for out, x in ((cand, tv), (cid, tf)):
                        for i0, ni, nj, p0 in STAIRS:
                            shp = [P, NT, ni, nj]
                            ins = v.tensor_tensor(out[:, :, p0:p0 + ni * nj].rearrange("p t (i j) -> p t i j", j=nj),
                                                  bc(x[0][:, :, i0:i0 + ni], 3, shp), bc(x[1][:, :, 0:nj], 2, shp), ALU.add)
                    dl_(ins)
                    top16(cand, bv, bp)
                    v.tensor_copy(gw[:, :, hs, :].rearrange("p t o k -> p t (o k)"), bv[:, :, :])
                    dl_(v.tensor_copy(bpf[:, :, :], bp[:, :, :]))
                    shp = [P, NT, TOPK, NCAND]
                    v.tensor_tensor(hot[:, :, :, :], iota[:, :].unsqueeze(1).unsqueeze(1).broadcast_to(shp), bc(bpf[:, :, :], 3, shp), ALU.is_equal).then_inc(pos_ready, 1)
                    v.wait_ge(hot_ready, h + 1)
                    dl_(v.tensor_reduce(eidf[:, :, hs, :].rearrange("p t o k -> p t (o k)"), hot[:, :, :, :], AX, ALU.add))
                    v.sem_inc(hot_used, 1)
                dl_.end(H)
                v.tensor_copy(eidx[:, :, :], eidf[:, :, :, :].rearrange("p t h k -> p t (h k)"))
                gv = gw[:, :, :, :].rearrange("p t h k -> p (t h) k")
                dl_(v.tensor_copy(gsum[:, :], gv[:, :, 0]))
                v.tensor_tensor(gv, gv, bc(gsum[:, :], 2, [P, NT * H, TOPK]), ALU.subtract).then_inc(max_ready, 1)
                v.wait_ge(exp_ready, 1)
                dl_(v.tensor_reduce(gsum[:, :], gv, AX, ALU.add))
                dl_(v.reciprocal(gsum[:, :], gsum[:, :]))
                dl_(v.tensor_tensor(gv, gv, bc(gsum[:, :], 2, [P, NT * H, TOPK]), ALU.mult))
        dl_.flat()
        gl_.flat()
        s3.close()
        late.close()

        rows = sb(ctx, "rows", [P, RING, D])
        slots = sb(ctx, "slots", [P, 2, RING], U32)
        htok, xtok = sb(ctx, "htok", [P, D]), sb(ctx, "xtok", [P, D])
        g2 = sb(ctx, "g2r", [P, D])
        fnw = sb(ctx, "fnw", [P, D])
        dots16, dots = sb(ctx, "dots16", [P, TOPK]), sb(ctx, "dots", [P, P])
        acc = sb(ctx, "acc", [P, D])
        yb, junk = sb(ctx, "yb", [P, D]), sb(ctx, "junk", [P, D])
        ss = sb(ctx, "ss", [P, 2])
        landed = [sem(f"landed{i}") for i in range(RING)]
        used, tile_in, tile_used, gelu_ready, dots_ready = (sem(n) for n in ("used", "tile_in", "tile_used", "gelu_ready", "dots_ready"))
        fin_in, y_ready, y_out, x3_ready, ss_ready, slot_ready, hused, g2s_in = (sem(n) for n in ("fin_in", "y_ready", "y_out", "x3_ready", "ss_ready", "slot_ready", "hused", "g2s_in"))
        GP = 2 * P
        NG = GP // RING

        with nc.Block() as block:
            @block.sync
            def _(sp):
                sp.dma_start(fnw[:, :], I["fnw"].partition_broadcast(P)).then_inc(fin_in, 16)
                sp.dma_start(g2[:, :], S["g2"][0]).then_inc(fin_in, 16)

                def load(t, rws):
                    ts_ = bass.ds(t, 1)
                    sp.dma_start(htok[0:rws, :], S["hn2"][ts_, 0:rws].rearrange("o p d -> p (o d)")).then_inc(tile_in, 16)
                    sp.dma_start(xtok[0:rws, :], S["x2"][ts_, 0:rws].rearrange("o p d -> p (o d)")).then_inc(tile_in, 16)
                load(0, P)
                with sp.Fori(1, NT - 1) as t:
                    sp.wait_ge(y_ready, t)
                    sp.dma_start(O["y_prompt"][bass.ds((t - 1) * P, P), :], yb[:, :]).then_inc(y_out, 16)
                    load(t, P)
                sp.wait_ge(y_ready, NT - 1)
                sp.dma_start(O["y_prompt"][SEQ - P:SEQ, :], yb[:, :]).then_inc(y_out, 16)
                load(NT - 1, TS)
                sp.dma_start(g2[0:TS, :], S["g2"][1, 0:TS]).then_inc(g2s_in, 16)
                sp.wait_ge(y_ready, NT)
                sp.dma_start(O["y_sample"][:, :], yb[0:TS, :]).then_inc(y_out, 16)
                sp.wait_ge(y_out, 16 * NT + 16)

            @block.gpsimd
            def _(g):
                def gathers(grp, h, col, t, table, rws):
                    g.wait_ge(used, grp * 8 + 8)
                    hold(g)
                    g.tensor_copy(slots[0:rws, h, :], eidx[0:rws, bass.ds(t, 1), bass.ds(col, RING)].rearrange("p o c -> p (o c)")).then_inc(slot_ready, 1)
                    g.wait_ge(slot_ready, grp + 1)
                    for s in range(RING):
                        g.wait_ge(used, grp * 8 + (s + 9))
                        hold(g)
                        g.indirect_dma_start(rows[0:rws, s, :], None, table[:, :], bass.IndirectOffsetOnAxis(ap=slots[0:rws, h, s:s + 1], axis=0)).then_inc(landed[s], 16)

                def tile(t, rws):
                    for ph, table in enumerate((I["peer_u"], I["peer_v"])):
                        with g.Fori(0, NG // 4) as i:
                            for h in range(2):
                                gathers(t * NG + i * 2 + (ph * NG // 2 + h), h, i * 16 + h * 8, t, table, rws)
                with g.Fori(0, NT - 1) as t:
                    tile(t, P)
                tile(NT - 1, TS)

            @block.vector
            def _(v):
                v.sem_inc(used, 16)
                v.sem_inc(y_out, 16)
                v.wait_ge(fin_in, 32)

                def tile(t, rws, ch1):
                    r = slice(0, rws)
                    v.wait_ge(tile_in, t * 32 + 32)
                    hold(v)
                    with v.Fori(0, NG // 4) as i:
                        for n in range(16):
                            s, h = n % 8, n // 8
                            v.wait_ge(landed[s], t * (16 * NG) + i * 32 + (16 * h + 16))
                            v.tensor_tensor_reduce(rows[r, s, :], rows[r, s, :], htok[r, :], 1.0, 0.0, ALU.mult, ALU.add, dots16[r, n:n + 1]).then_inc(used, 1)
                        v.wait_ge(used, t * GP + i * 16 + 32)
                        v.tensor_copy(dots[r, bass.ts(i, 16)], dots16[r, :]).then_inc(dots_ready, 1)
                        v.wait_ge(dots_ready, t * 8 + i + 1)
                    v.wait_ge(gelu_ready, t + 1)
                    v.tensor_tensor(dots[r, :], dots[r, :], gw[r, bass.ds(t, 1), :, :].rearrange("p o h k -> p (o h k)"), ALU.mult)
                    ch1(v.memset(acc[r, :], 0.0))
                    hold(v)
                    with v.Fori(0, NG // 4) as i:
                        for n in range(16):
                            s, h = n % 8, n // 8
                            v.wait_ge(used, t * GP + i * 16 + (P + 16 + n))
                            v.wait_ge(landed[s], t * (16 * NG) + i * 32 + (16 * h + 16 + 8 * NG))
                            v.scalar_tensor_tensor(acc[r, :], rows[r, s, :], dots[r, bass.ds(i * 16 + n, 1)], acc[r, :], ALU.mult, ALU.add).then_inc(used, 1)
                    v.wait_ge(used, t * GP + (GP + 16))
                    ch1(v.tensor_tensor(acc[r, :], acc[r, :], g2[r, :], ALU.mult))
                    v.tensor_tensor(acc[r, :], acc[r, :], xtok[r, :], ALU.add).then_inc(x3_ready, 1)
                    v.wait_ge(ss_ready, t + 1)
                    ch1(v.reciprocal(ss[r, 1:2], ss[r, 1:2]))
                    v.wait_ge(y_out, t * 16 + 16)
                    v.scalar_tensor_tensor(yb[r, :], acc[r, :], ss[r, 1:2], fnw[r, :], ALU.mult, ALU.mult).then_inc(y_ready, 1)
                    v.wait_ge(y_ready, t + 1)
                with v.Fori(0, NT - 1) as t:
                    dl_.loop(t, 3)
                    tile(t, P, dl_)
                dl_.end(NT - 1)
                v.wait_ge(g2s_in, 16)
                tile(NT - 1, TS, dl_)
                dl_.flat()

            @block.scalar
            def _(act):
                def tile(t, rws, link):
                    r = slice(0, rws)
                    act.wait_ge(dots_ready, t * 8 + 8)
                    act.activation(dots[r, :], dots[r, :], ACT.Gelu_apprx_tanh).then_inc(gelu_ready, 1)
                    act.wait_ge(x3_ready, t + 1)
                    link(act.activation(junk[r, :], acc[r, :], ACT.Square, accum_out=ss[r, 0:1]))
                    act.activation(ss[r, 1:2], ss[r, 0:1], ACT.Sqrt, bias=epsb[r, 0:1], scale=1.0 / D).then_inc(ss_ready, 1)
                with act.Fori(0, NT - 1) as t:
                    al_.loop(t, 1)
                    tile(t, P, al_)
                al_.end(NT - 1)
                tile(NT - 1, TS, al_)
                al_.flat()


OUTS = {
    "y_prompt": (SEQ, D), "y_sample": (TS, D), "ret_prompt": (H, DK, P), "ret_sample": (NB, H, DK, P),
    "conv": (P, KC, (1 + NB) * HIST), "lru": (P, KC, 1 + NB),
}
SCRATCH = {"g2": (2, P, D), "mg": (KC, P, T), "x2": (NT, P, D), "hn2": (NT, P, D)}


def kernel(**inputs):
    import concourse.bacc as bacc
    from concourse.bass_utils import run_bass_kernel_spmd as run

    a = {k: np.asarray(v) for k, v in inputs.items()}

    def chunks(x):
        return x.reshape(-1, KC, P).transpose(2, 1, 0)

    x = np.concatenate([a["x_prompt"].reshape(SEQ, D), a["x_sample"].reshape(TS, D)])
    c = np.concatenate([a["c_prompt"], a["c_sample"]])
    w = a["w_in"][0]
    cuts = [w[:, i * 64:(i + 1) * 64] for i in range(16)]
    rest = [[w[:, 1024 + g * 1024 + f * P:1024 + g * 1024 + (f + 1) * P] for f in range(KC)] for g in range(6)]
    v_, g_ret, x_lru, g_lru, gate_a, gate_b = rest
    w_in = np.stack([np.concatenate([cuts[f], cuts[8 + f], v_[f], x_lru[f], g_lru[f], g_ret[f], gate_a[f], gate_b[f]], axis=1) for f in range(KC)])
    vecs = np.concatenate([a["norm1_w"], a["norm2_w"], a["ret_gn_w"], a["conv_b"], a["conv_w"][0], a["lru_ba"], a["lru_bx"], a["lru_lambda"]])
    wax = np.stack([a["lru_wa"][0], a["lru_wx"][0]], axis=2).reshape(KC, P, 2, 64)
    arrays = {
        "xT": x.T, "cT": chunks(c), "w_ada": a["w_ada"][0], "bada": a["b_ada"].reshape(48, P).T,
        "b_g2": a["b_ada"][0, 5 * D:].reshape(D), "vec": vecs.reshape(NVEC, KC, P).transpose(2, 0, 1), "w_in": w_in, "wax": wax,
        "state_ret": a["state_ret"][0], "h0": chunks(a["state_lru"][0]),
        "c0": a["state_conv"][0].reshape(NB * HIST, KC, P).transpose(2, 1, 0),
        "w_out": a["w_out"][0], "peer_wq": a["peer_wq"][0],
        "keys": np.stack([a["peer_k1"][0].T, a["peer_k2"][0].T], axis=1),
        "peer_u": a["peer_u"][0], "peer_v": a["peer_v"][0], "fnw": a["final_norm_w"],
    }
    arrays = {k: np.ascontiguousarray(v) for k, v in arrays.items()}
    arrays.update(tables())
    nc = bacc.Bacc("TRN2", target_bir_lowering=False, num_devices=1)
    I = {k: nc.dram_tensor(f"in_{k}", v.shape, F32, kind="ExternalInput").ap() for k, v in arrays.items()}
    O = {k: nc.dram_tensor(f"out_{k}", s, F32, kind="ExternalOutput").ap() for k, s in OUTS.items()}
    S = {k: nc.dram_tensor(f"scratch_{k}", s, F32, kind="Internal").ap() for k, s in SCRATCH.items()}
    program(nc, I, O, S)
    r = run(nc, [{f"in_{k}": v for k, v in arrays.items()}], core_ids=[0]).results[0]
    o = {k: r[f"out_{k}"] for k in OUTS}
    conv = o["conv"].reshape(P, KC, 1 + NB, HIST).transpose(2, 3, 1, 0).reshape(1 + NB, HIST, D)
    lru = o["lru"].transpose(2, 1, 0).reshape(1 + NB, D)
    return (o["y_prompt"].reshape(1, SEQ, D), o["y_sample"].reshape(NB, NS, D), o["ret_prompt"].reshape(1, 1, H, DK, P),
            lru[None, 0:1], conv[None, 0:1], o["ret_sample"].reshape(1, NB, H, DK, P), lru[None, 1:], conv[None, 1:])
```

```python
from contextlib import ExitStack

import numpy as np
import concourse.bass as bass
from concourse import mybir

F32 = mybir.dt.float32
U32 = mybir.dt.uint32
BF16 = mybir.dt.bfloat16
ALU = mybir.AluOpType
ACT = mybir.ActivationFunctionType
AX = mybir.AxisListType.X

P = 128
D = 1024
KC = D // P
SEQ = 1024
NB, NS = 8, 8
TS = NB * NS
T = SEQ + TS
NT = SEQ // P + 1
TPAD = NT * P
H = 8
DK = 64
CONV = 4
HIST = CONV - 1
XR = HIST + SEQ
CW = DK + DK + P
SLAB = CW + 5 * P
TOPK = 16
NKEY = 128
EPS = 1e-6
PAST = 8192
SLICES = ((0, 512), (512, 1024), (1024, T))
STAIRS = ((0, 1, 16, 0), (1, 1, 8, 16), (2, 2, 5, 24), (4, 4, 3, 34), (8, 8, 1, 46))
NCAND = 54
SUMW = 14
TPOOL = 3
ADA_W = 512
ADA_CH = ADA_W // P
NSLAB = 6 * D // ADA_W
NMOD = 6 * KC
SH1, SC1, G1, SH2, SC2, G2 = 0, 8, 16, 24, 32, 40
V_N1, V_N2, V_GN, V_CB, V_CW, V_BA, V_BX, V_LAM, V_FN, NVEC = 0, 1, 2, 3, 4, 8, 9, 10, 11, 12
LOW = -3.0e38


def tables():
    t = np.zeros((TPAD,), np.float32)
    t[:SEQ] = np.arange(SEQ)
    t[SEQ:T] = PAST + np.arange(TS) % NS
    half = DK // 2
    inv = np.power(np.float32(10000.0), -np.arange(half, dtype=np.float32) / np.float32(half)).astype(np.float32)
    ang = (t[:, None] * inv[None]).astype(np.float32).astype(np.float64)
    cos, sin = np.cos(ang), np.sin(ang)
    rope_c = np.concatenate([cos, cos], 1).reshape(NT, P, DK).transpose(1, 0, 2)
    rope_s = np.concatenate([-sin, sin], 1).reshape(NT, P, DK).transpose(1, 0, 2)
    lg = np.log1p(-np.exp2(-5.0 - np.arange(H)))
    n = np.arange(P)
    diff = n[None, :] - n[:, None]
    mask = np.where(diff[None] >= 0, np.exp(np.maximum(diff, 0)[None] * lg[:, None, None]), 0.0)
    m = np.arange(TS)
    sdiff = m[None, :] - m[:, None]
    same = (m[None, :] // NS == m[:, None] // NS) & (sdiff >= 0)
    smask = np.where(same[None], np.exp(np.maximum(sdiff, 0)[None] * lg[:, None, None]), 0.0)
    xi = np.exp((n[None, :] + 1.0) * lg[:, None])
    scale = DK ** -0.5
    zeta = np.exp((P - 1.0 - n[:, None]) * lg[None]) * scale
    szeta = np.exp((NS - 1.0 - (m % NS)[:, None, None]) * lg[None, :, None]) * scale
    szeta = szeta * (m[:, None, None] // NS == np.arange(NB)[None, None, :])
    gch = np.stack([np.exp(P * lg), np.exp(NS * lg)])
    c = {
        "rope_c": rope_c, "rope_s": rope_s,
        "dmask": mask.transpose(1, 0, 2), "smask": smask.transpose(1, 0, 2),
        "xi": np.broadcast_to(xi[None], (DK, H, P)),
        "zeta": zeta, "szeta": szeta,
        "gch": np.broadcast_to(gch[None], (DK, 2, H)),
        "ident": np.eye(P),
        "iota": np.broadcast_to(np.arange(P)[None], (P, P)),
    }
    return {k: np.ascontiguousarray(v, dtype=np.float32) for k, v in c.items()}


class Chain:

    def __init__(self, eng, sem):
        self.eng, self.sem, self.base, self.k, self.off = eng, sem, 0, 0, None

    def __call__(self, ins):
        self.k += 1
        ins.then_inc(self.sem, 1)
        at = self.base + self.k
        self.eng.wait_ge(self.sem, at if self.off is None else self.off + at)

    def loop(self, i, per):
        self.flat()
        self.off, self.per = i * per, per

    def end(self, n):
        assert self.k == self.per, f"{self.k} links in the loop's body"
        self.base, self.k, self.off = self.base + n * self.per, 0, None

    def flat(self):
        self.base, self.k = self.base + self.k, 0


def program(nc, I, O, S):
    ctx = ExitStack()

    def sem(name):
        return ctx.enter_context(nc.semaphore(name))

    def sb(c, name, shape, dt=F32):
        return c.enter_context(nc.sbuf_tensor(name, shape, dt))

    def bc(ap, axis, shape):
        return ap.unsqueeze(axis).broadcast_to(shape)

    hold_sem = sem("hold")

    def hold(eng):
        eng.sem_inc(hold_sem, 1)

    with ctx:
        early = ExitStack()
        pj = early.enter_context(nc.psum_tensor("pj", [P, 1536], F32))
        pk = early.enter_context(nc.psum_tensor("pk", [P, 1536], F32))
        R = [early.enter_context(nc.psum_tensor(f"r{i}", [P, 512], F32)) for i in range(2)]

        dve_chain, act_chain, pool_chain = sem("dve_chain"), sem("act_chain"), sem("pool_chain")
        dl_ = Chain(nc.vector, dve_chain)
        al_ = Chain(nc.scalar, act_chain)
        gl_ = Chain(nc.gpsimd, pool_chain)

        g2T, fnw = sb(ctx, "g2T", [P, KC, 1 + NB]), sb(ctx, "fnw", [P, KC])
        ones = sb(ctx, "ones", [P, P])
        ident = sb(ctx, "ident", [P, P])
        eidx = sb(ctx, "eidx", [P, NT, P], U32)
        gw = sb(ctx, "gw", [P, NT, H, TOPK])
        iota = sb(ctx, "iota", [P, P])
        epsb = sb(ctx, "epsb", [P, 1])

        mods = ExitStack()
        vec = sb(mods, "vec", [P, NVEC, KC])
        modT = sb(mods, "modT", [P, NMOD, 1 + NB])

        mix = ExitStack()
        onesm = sb(mix, "onesm", [P, P])
        coef = sb(mix, "coef", [P, KC])
        hnT = sb(mix, "hnT", [P, KC, TPAD])
        w_qkv = sb(mix, "w_qkv", [P, KC, CW])
        w_part = [sb(mix, f"w_part{j}", [P, KC, P]) for j in range(5)]
        wab = sb(mix, "wab", [P, 2, P])

        w_in_sems = [sem(f"w_in{j}") for j in range(6)]
        wab_in, wo_in = sem("wab_in"), sem("wo_in")
        wo = hnT[:, :, 0:D]
        scaled = sem("scaled")

        def adjust(eng_chain, x, out, rstd, gain, shift, tmp):
            v = nc.vector
            for k in range(KC):
                v.scalar_tensor_tensor(out[:, k, 0:SEQ], x[:, k, 0:SEQ], gain[:, k, 0:1], rstd[:, 0:SEQ], ALU.mult, ALU.mult).then_inc(scaled, 1)
            ins2 = v.tensor_tensor(tmp[:, :, :], x[:, :, SEQ:T], bc(rstd[:, SEQ:T], 1, [P, KC, TS]), ALU.mult)
            eng_chain(ins2)
            t4 = tmp[:, :, :].rearrange("p k (b t) -> p k b t", t=NS)
            o4 = out[:, :, SEQ:T].rearrange("p k (b t) -> p k b t", t=NS)
            eng_chain(v.tensor_tensor(t4, t4, bc(gain[:, :, 1:1 + NB], 3, [P, KC, NB, NS]), ALU.mult))
            eng_chain(v.tensor_tensor(o4, t4, bc(shift[:, :, 1:1 + NB], 3, [P, KC, NB, NS]), ALU.add))

        def add_shift(out, shift, before):
            for k in range(KC):
                nc.scalar.wait_ge(scaled, before + k + 1)
                nc.scalar.activation(out[:, k, 0:SEQ], out[:, k, 0:SEQ], ACT.Identity, bias=shift[:, k, 0:1])

        s0 = ExitStack()
        xT = sb(s0, "xT", [P, KC, T])
        cT = sb(s0, "cT", [P, KC, 1 + NB])
        scT = sb(s0, "scT", [P, KC, 1 + NB])
        bada = sb(s0, "bada", [P, 48])
        ada = [sb(s0, f"ada{u}", [P, KC, ADA_W]) for u in range(2)]
        row = [sb(s0, f"row{u}", [1 + NB, ADA_W]) for u in range(2)]
        sq = [sb(s0, f"sq{u}", [P, T]) for u in range(2)]
        rstd = sb(s0, "rstd", [P, T])
        gain = sb(s0, "gain", [P, KC, 1 + NB])
        tmp0 = sb(s0, "tmp0", [P, KC, TS])
        lam = [sb(s0, f"lam{i}", [P, KC]) for i in range(5)]

        x_in, small_in, ada_in = sem("x_in"), sem("small_in"), [sem("ada_in0"), sem("ada_in1")]
        ada_used, mod_ps, mod_read = sem("ada_used"), sem("mod_ps"), sem("mod_read")
        sc_ready, row_ready, row_turned = sem("sc_ready"), sem("row_ready"), sem("row_turned")
        sq_ready, sq_used, ssum_ready, sd_ready = sem("sq_ready"), sem("sq_used"), sem("ssum_ready"), sem("sd_ready")
        ones_ready, e_ready, u_ready, ln_ready = sem("ones_ready"), sem("e_ready"), sem("u_ready"), sem("ln_ready")

        def w_in_load(sp, f, j):
            a, b = (0, CW) if j == 0 else (CW + (j - 1) * P, CW + j * P)
            dst = w_qkv if j == 0 else w_part[j - 1]
            src = I["w_in"][bass.ds(f, 1), :, a:b].rearrange("o (k p) n -> p (o k) n", p=P)
            sp.dma_start(dst[:, :, :], src).then_inc(w_in_sems[j], 16)

        def wab_load(sp, f):
            for q in range(2):
                src = I["wax"][bass.ds(f, 1), 64 * q:64 * q + 64].rearrange("o p a e -> p (o a) e")
                sp.dma_start(wab[64 * q:64 * q + 64, :, 64 * q:64 * q + 64], src).then_inc(wab_in, 16)

        with nc.Block() as block:
            @block.sync
            def _(sp):
                def ada_load(s, u):
                    sp.dma_start(ada[u][:, :, :], I["w_ada"][:, bass.ts(s, ADA_W)].rearrange("(k p) n -> p k n", p=P)).then_inc(ada_in[u], 16)
                for dst, src in ((cT, "cT"), (vec, "vec"), (bada, "bada"), (ident, "ident")):
                    sp.dma_start(dst[:], I[src]).then_inc(small_in, 16)
                sp.dma_start(xT[:, :, :], I["xT"].rearrange("(k p) t -> p k t", p=P)).then_inc(x_in, 16)
                ada_load(0, 0)
                ada_load(1, 1)
                with sp.Fori(1, NSLAB // 2) as i:
                    for u in range(2):
                        sp.wait_ge(ada_used, i * 2 + (u - 1))
                        ada_load(i * 2 + u, u)
                sp.wait_ge(ones_ready, 4)
                wab_load(sp, 0)
                for j in range(6):
                    w_in_load(sp, 0, j)

            @block.scalar
            def _(act):
                act.wait_ge(small_in, 64)
                act.activation(scT[:, :, :], cT[:, :, :], ACT.Silu).then_inc(sc_ready, 1)
                al_(act.activation(lam[0][:, :], vec[:, V_LAM, :], ACT.Abs))
                act.activation(lam[1][:, :], lam[0][:, :], ACT.Exp, scale=-1.0).then_inc(e_ready, 1)
                act.wait_ge(u_ready, 1)
                act.activation(lam[3][:, :], lam[2][:, :], ACT.Ln).then_inc(ln_ready, 1)
                act.wait_ge(x_in, 16)
                for k in range(KC):
                    if k >= 2:
                        act.wait_ge(sq_used, k - 1)
                    act.activation(sq[k % 2][:, :], xT[:, k, :], ACT.Square).then_inc(sq_ready, 1)
                act.wait_ge(ssum_ready, 1)
                act.wait_ge(ones_ready, 4)
                act.activation(rstd[:, :], pj[:, 0:T], ACT.Sqrt, bias=epsb[:, 0:1], scale=1.0 / D).then_inc(sd_ready, 1)
                act.sem_inc(row_turned, 2)
                with act.Fori(0, NSLAB // 2) as i:
                    for u in range(2):
                        act.wait_ge(mod_ps, i * 2 + (u + 1))
                        act.wait_ge(row_turned, i * 2 + (u + 1))
                        act.activation(row[u][0:1 + NB, :], R[u][0:1 + NB, 0:ADA_W], ACT.Copy).then_inc(row_ready, 1)
                add_shift(hnT, modT[:, SH1:SH1 + 8, :], 0)

            @block.tensor
            def _(pe):
                pe.wait_ge(ones_ready, 4)
                for k in range(KC):
                    pe.wait_ge(sq_ready, k + 1)
                    for a, b in SLICES:
                        mm = pe.matmul(pj[:, a:b], ones[:, :], sq[k % 2][:, a:b], start=(k == 0), stop=(k == KC - 1))
                    mm.then_inc(sq_used, 1)
                pe.wait_ge(sq_used, KC)
                pe.sem_inc(ssum_ready, 1)
                pe.wait_ge(sc_ready, 1)

                pe.sem_inc(mod_read, 2)

                def slab(i, u, first):
                    pe.wait_ge(ada_in[u], i * 16 + 16)
                    if not first:
                        pe.wait_ge(row_ready, i * 2 + (u - 1))
                    for k in range(KC):
                        mm = pe.matmul(R[u][0:1 + NB, 0:ADA_W], scT[:, k, :], ada[u][:, k, :], start=(k == 0), stop=(k == KC - 1))
                    mm.then_inc(mod_ps, 1)

                def turn(s, u):
                    pe.wait_ge(row_ready, s + 1)
                    pe.sem_inc(ada_used, 1)
                    pe.wait_ge(mod_read, s + 1)
                    hold(pe)
                    for m in range(ADA_CH):
                        mm = pe.transpose(pk[:, u * 512 + m * 9:u * 512 + (m + 1) * 9], row[u][0:1 + NB, m * P:(m + 1) * P], ident[0:1 + NB, 0:1 + NB])
                    mm.then_inc(row_turned, 1)
                slab(0, 0, True)
                slab(0, 1, True)
                turn(0, 0)
                with pe.Fori(1, NSLAB // 2) as i:
                    slab(i, 0, False)
                    turn(i * 2 - 1, 1)
                    slab(i, 1, False)
                    turn(i * 2, 0)
                turn(NSLAB - 1, 1)

            @block.vector
            def _(v):
                v.memset(ones[:, :], 1.0).then_inc(ones_ready, 1)
                v.memset(onesm[:, :], 1.0 / P).then_inc(ones_ready, 1)
                v.memset(wab[:, :, :], 0.0).then_inc(ones_ready, 1)
                v.memset(epsb[:, :], EPS).then_inc(ones_ready, 1)
                v.memset(hnT[:, :, T:TPAD], 0.0)
                v.wait_ge(e_ready, 1)
                v.tensor_scalar(lam[2][:, :], lam[1][:, :], 1.0, None, ALU.add).then_inc(u_ready, 1)
                v.wait_ge(u_ready, 1)
                dl_(v.tensor_scalar(lam[4][:, :], lam[2][:, :], -1.0, None, ALU.add))
                dl_(v.tensor_tensor(lam[4][:, :], lam[1][:, :], lam[4][:, :], ALU.subtract))
                dl_(v.reciprocal(coef[:, :], lam[2][:, :]))
                dl_(v.tensor_tensor(lam[4][:, :], lam[4][:, :], coef[:, :], ALU.mult))
                v.wait_ge(ln_ready, 1)
                dl_(v.tensor_tensor(lam[4][:, :], lam[4][:, :], lam[3][:, :], ALU.add))
                dl_(v.tensor_scalar(coef[:, :], vec[:, V_LAM, :], -1.0, 0.0, ALU.mult, ALU.max))
                dl_(v.tensor_tensor(lam[4][:, :], lam[4][:, :], coef[:, :], ALU.add))
                dl_(v.tensor_scalar(coef[:, :], lam[4][:, :], -8.0, None, ALU.mult))
                v.wait_ge(sd_ready, 1)
                dl_(v.reciprocal(rstd[:, :], rstd[:, :]))

                def mod(i, u):
                    s = i * 2 + u
                    v.wait_ge(row_turned, s + 3)
                    v.tensor_tensor(modT[:, bass.ds(s * ADA_CH, ADA_CH), :], pk[:, u * 512:u * 512 + 9 * ADA_CH].rearrange("p (m c) -> p m c", c=9),
                                    bc(bada[:, bass.ds(s * ADA_CH, ADA_CH)], 2, [P, ADA_CH, 9]), ALU.add).then_inc(mod_read, 1)
                with v.Fori(0, NSLAB // 2) as i:
                    mod(i, 0)
                    mod(i, 1)
                v.wait_ge(mod_read, NSLAB + 2)
                dl_(v.scalar_tensor_tensor(gain[:, :, :], modT[:, SC1:SC1 + 8, :], 1.0, bc(vec[:, V_N1, :], 2, [P, KC, 9]), ALU.add, ALU.mult))
                adjust(dl_, xT, hnT, rstd, gain, modT[:, SH1:SH1 + 8, :], tmp0)
        for ch in (dl_, al_, gl_):
            ch.flat()
        s0.close()

        s1 = ExitStack()
        rope_c, rope_s = sb(s1, "rope_c", [P, NT, DK]), sb(s1, "rope_s", [P, NT, DK])
        dmask, smask = sb(s1, "dmask", [P, H, P]), sb(s1, "smask", [TS, H, TS])
        xi, zeta, szeta = sb(s1, "xi", [DK, H, P]), sb(s1, "zeta", [P, H]), sb(s1, "szeta", [TS, H, NB])
        gch = sb(s1, "gch", [DK, 2, H])
        h0, c0 = sb(s1, "h0", [P, KC, NB]), sb(s1, "c0", [P, KC, NB * HIST])
        tok = sb(s1, "tok", [P, NT, CW])
        qkr = sb(s1, "qkr", [P, NT, 2, DK])
        rt = sb(s1, "rt", [P, NT, 2, DK])
        qT, kT, qxi = sb(s1, "qT", [DK, TPAD]), sb(s1, "kT", [DK, TPAD]), sb(s1, "qxi", [DK, T])
        pT, pTs = sb(s1, "pT", [P, NT - 1, P]), sb(s1, "pTs", [TS, TS])
        kz, kzb = sb(s1, "kz", [P, NT - 1, DK]), sb(s1, "kzb", [TS, NB, DK])
        Sall = sb(s1, "Sall", [DK, NT, P])
        S0, Sout = sb(s1, "S0", [DK, NB, P]), sb(s1, "Sout", [DK, NB, P])
        xr = sb(s1, "xr", [P, XR + NB * (HIST + NS)])
        xl, rg, ig, th, om = (sb(s1, n, [P, T]) for n in ("xl", "rg", "ig", "th", "om"))
        AS = SEQ + NB * (NS + 1)
        la, lb, lh = (sb(s1, n, [P, AS]) for n in ("la", "lb", "lh"))
        glru, gret, gate = (sb(s1, n, [P, T]) for n in ("glru", "gret", "gate"))
        osb, dsq = sb(s1, "osb", [P, T]), sb(s1, "dsq", [P, T])
        convo, lruo = sb(s1, "convo", [P, KC, (1 + NB) * HIST]), sb(s1, "lruo", [P, KC, 1 + NB])

        def seqs(ap, w):
            return ap.rearrange("p (b t) -> p b t", t=w)

        xrs = seqs(xr[:, XR:], HIST + NS)
        las, lbs, lhs_ = (seqs(t[:, SEQ:], NS + 1) for t in (la, lb, lh))

        tab_in, S0_in, S0_used = sem("tab_in"), sem("S0_in"), sem("S0_used")
        pj_ready, pk_ready, pj_free, pk_free = sem("pj_ready"), sem("pk_ready"), sem("pj_free"), sem("pk_free")
        w_used = [sem(f"w_used{j}") for j in range(6)]
        wab_used = sem("wab_used")
        st_ready, st_free, var_free = sem("st_ready"), sem("st_free"), sem("var_free")
        qkv_ready, xr_ready, xr_used = sem("qkv_ready"), sem("xr_ready"), sem("xr_used")
        rope_ready, glru_ready, gret_ready, ga_ready, ga_used, gb_ready = (sem(n) for n in ("rope_ready", "glru_ready", "gret_ready", "ga_ready", "ga_used", "gb_ready"))
        xl_ready, r_ready, i_ready, th_ready, a_ready, m2_ready, mult_ready = (sem(n) for n in ("xl_ready", "r_ready", "i_ready", "th_ready", "a_ready", "m2_ready", "mult_ready"))
        qkT_ready, pT_ready, kz_ready, S_ready, Sout_ready, o_ready, d_ready, dsq_ready, sdv_ready = (sem(n) for n in ("qkT_ready", "pT_ready", "kz_ready", "S_ready", "Sout_ready", "o_ready", "d_ready", "dsq_ready", "sdv_ready"))
        mg_ready, mg_out, st_out, lo_out, f_done = (sem(n) for n in ("mg_ready", "mg_out", "st_out", "lo_out", "f_done"))
        NST, NVAR = 18, 3

        with nc.Block() as block:
            @block.sync
            def _(sp):
                for dst, src in ((rope_c, "rope_c"), (rope_s, "rope_s"), (dmask, "dmask"), (smask, "smask"), (xi, "xi"),
                                 (zeta, "zeta"), (szeta, "szeta"), (gch, "gch"), (h0, "h0"), (c0, "c0")):
                    sp.dma_start(dst[:], I[src]).then_inc(tab_in, 16)

                def s0_load(f):
                    src = I["state_ret"][:, bass.ds(f, 1)].rearrange("b o k v -> k (b o) v")
                    sp.dma_start(S0[:, :, :], src).then_inc(S0_in, 16)
                s0_load(0)

                def group(f, last):
                    if not last:
                        for j in range(6):
                            sp.wait_ge(w_used[j], f + 1)
                            w_in_load(sp, f + 1, j)
                        sp.wait_ge(wab_used, f + 1)
                        wab_load(sp, f + 1)
                    sp.wait_ge(S_ready, f + 1)
                    sp.dma_start(O["ret_prompt"][bass.ds(f, 1)].rearrange("o k v -> k (o v)"), Sall[:, NT - 1, :]).then_inc(st_out, 16)
                    sp.wait_ge(Sout_ready, f * 2 + 2)
                    sp.dma_start(O["ret_sample"][:, bass.ds(f, 1)].rearrange("b o k v -> k (b o) v"), Sout[:, :, :]).then_inc(st_out, 16)
                    if not last:
                        sp.wait_ge(S0_used, f + 1)
                        s0_load(f + 1)
                    else:
                        sp.wait_ge(w_used[5], f + 1)
                        sp.dma_start(wo, I["w_out"].rearrange("(k p) n -> p k n", p=P)).then_inc(wo_in, 16)
                    sp.wait_ge(mg_ready, f + 1)
                    sp.dma_start(S["mg"][bass.ds(f, 1)].rearrange("o p t -> p (o t)"), osb[:, :]).then_inc(mg_out, 16)
                with sp.Fori(0, H - 1) as f:
                    group(f, False)
                group(H - 1, True)
                sp.dma_start(O["conv"], convo[:, :, :]).then_inc(lo_out, 16)
                sp.dma_start(O["lru"], lruo[:, :, :]).then_inc(lo_out, 16)
                sp.wait_ge(lo_out, 32)
                sp.wait_ge(st_out, 32 * H + 32)
                sp.wait_ge(mg_out, 16 * H + 16)

            @block.scalar
            def _(act):
                act.sem_inc(pj_free, 1)
                act.sem_inc(pk_free, 1)
                act.sem_inc(var_free, 1)
                act.wait_ge(tab_in, 160)
                with act.Fori(0, H) as f:
                    fs = bass.ds(f, 1)
                    act.wait_ge(pj_ready, f * 5 + 1)
                    act.activation(tok[:, 0:6, :], pj[:, :].rearrange("p (t c) -> p t c", c=CW), ACT.Copy).then_inc(pj_free, 1)
                    act.wait_ge(pk_ready, f * 4 + 1)
                    act.activation(tok[:, 6:9, :], pk[:, 0:3 * CW].rearrange("p (t c) -> p t c", c=CW), ACT.Copy).then_inc(qkv_ready, 1)
                    act.wait_ge(qkv_ready, f + 1)
                    act.sem_inc(pk_free, 1)
                    act.wait_ge(pj_ready, f * 5 + 2)
                    act.wait_ge(xr_used, f + 1)
                    act.activation(xr[:, HIST:XR], pj[:, 0:SEQ], ACT.Copy)
                    act.activation(xrs[:, :, 0:HIST], c0[:, fs, :].rearrange("p o (b j) -> p (o b) j", j=HIST), ACT.Copy)
                    act.activation(xrs[:, :, HIST:], seqs(pj[:, SEQ:T], NS), ACT.Copy).then_inc(xr_ready, 1)
                    act.wait_ge(xr_ready, f + 1)
                    act.sem_inc(pj_free, 1)
                    act.wait_ge(pk_ready, f * 4 + 2)
                    act.wait_ge(f_done, f + 1)
                    act.activation(glru[:, :], pk[:, 0:T], ACT.Gelu_apprx_tanh).then_inc(glru_ready, 1)
                    act.wait_ge(glru_ready, f + 1)
                    act.sem_inc(pk_free, 1)
                    act.wait_ge(pj_ready, f * 5 + 3)
                    act.activation(gret[:, :], pj[:, 0:T], ACT.Silu).then_inc(gret_ready, 1)
                    act.wait_ge(gret_ready, f + 1)
                    act.sem_inc(pj_free, 1)
                    act.wait_ge(pk_ready, f * 4 + 3)
                    act.activation(gate[:, :], pk[:, 0:T], ACT.Sigmoid).then_inc(ga_ready, 1)
                    act.wait_ge(ga_ready, f + 1)
                    act.sem_inc(pk_free, 1)
                    act.wait_ge(pj_ready, f * 5 + 4)
                    act.activation(rg[:, :], pj[:, 0:T], ACT.Sigmoid, bias=vec[:, V_BA, fs]).then_inc(r_ready, 1)
                    act.wait_ge(r_ready, f + 1)
                    act.sem_inc(pj_free, 1)
                    act.wait_ge(pk_ready, f * 4 + 4)
                    act.wait_ge(ga_used, f + 1)
                    act.activation(gate[:, :], pk[:, 0:T], ACT.Sigmoid).then_inc(gb_ready, 1)
                    act.wait_ge(gb_ready, f + 1)
                    act.sem_inc(pk_free, 1)
                    act.wait_ge(pj_ready, f * 5 + 5)
                    act.activation(ig[:, :], pj[:, 0:T], ACT.Sigmoid, bias=vec[:, V_BX, fs]).then_inc(i_ready, 1)
                    act.wait_ge(i_ready, f + 1)
                    act.sem_inc(pj_free, 1)
                    act.activation(th[:, :], rg[:, :], ACT.Tanh, scale=coef[:, fs]).then_inc(th_ready, 1)
                    act.activation(la[:, 0:SEQ], rg[:, 0:SEQ], ACT.Exp, scale=coef[:, fs])
                    act.activation(las[:, :, 1:], seqs(rg[:, SEQ:T], NS), ACT.Exp, scale=coef[:, fs]).then_inc(a_ready, 1)
                    act.wait_ge(m2_ready, f + 1)
                    act.activation(om[:, :], om[:, :], ACT.Sqrt).then_inc(mult_ready, 1)
                    act.wait_ge(d_ready, f + 1)
                    act.activation(dsq[:, :], osb[:, :], ACT.Square).then_inc(dsq_ready, 1)
                    for n, (a, b) in enumerate(SLICES):
                        act.wait_ge(st_ready, f * (NST + NVAR) + NST + 1 + n)
                        act.activation(dsq[:, a:b], R[n % 2][:, 0:b - a], ACT.Sqrt, bias=epsb[:, 0:1]).then_inc(sdv_ready, 1)
                    act.wait_ge(sdv_ready, f * 3 + 3)
                    act.sem_inc(var_free, 1)

            @block.tensor
            def _(pe):
                pe.wait_ge(tab_in, 160)
                def qkv_tiles(f, bank, tiles, free, ready):
                    pe.wait_ge(*free)
                    for t in tiles:
                        dst = bank[:, (t - tiles[0]) * CW:(t - tiles[0] + 1) * CW]
                        for k in range(KC):
                            mm = pe.matmul(dst, hnT[:, k, t * P:(t + 1) * P], w_qkv[:, k, :], start=(k == 0), stop=(k == KC - 1))
                    mm.then_inc(ready, 1)

                def qkv_high(f):
                    pe.wait_ge(w_in_sems[0], f * 16 + 16)
                    qkv_tiles(f, pk, range(6, NT), (pk_free, f * 4 + 1), pk_ready)

                def qkv_low(f):
                    qkv_tiles(f, pj, range(0, 6), (pj_free, f * 5 + 1), pj_ready)
                    pe.wait_ge(pj_ready, f * 5 + 1)
                    pe.sem_inc(w_used[0], 1)

                def head(f, last):
                    use = {"pj": 1, "pk": 1}

                    def bank_wait(b):
                        pe.wait_ge(pj_free if b == "pj" else pk_free, f * (5 if b == "pj" else 4) + use[b] + 1)
                        use[b] += 1
                    def part(j, b, s, ready, count):
                        if s == 0:
                            pe.wait_ge(w_in_sems[j], f * 16 + 16)
                            bank_wait(b)
                        a, e = SLICES[s]
                        for k in range(KC):
                            mm = pe.matmul((pj if b == "pj" else pk)[:, a:e], w_part[j - 1][:, k, :], hnT[:, k, a:e], start=(k == 0), stop=(k == KC - 1))
                        if s == 2:
                            mm.then_inc(ready, 1)
                            pe.wait_ge(ready, count)
                            pe.sem_inc(w_used[j], 1)

                    def lru_gate(g, b, ready):
                        bank_wait(b)
                        for a, e in SLICES:
                            mm = pe.matmul((pj if b == "pj" else pk)[:, a:e], wab[:, g, :], xl[:, a:e], start=True, stop=True)
                        mm.then_inc(ready, 1)

                    st = [0]

                    def stage_wait():
                        n = st[0]
                        if n < 2:
                            pe.wait_ge(var_free, f + 1)
                        elif n <= NST + 1:
                            pe.wait_ge(st_free, f * NST + (n - 1))
                        else:
                            pe.wait_ge(sdv_ready, f * 3 + 1)
                        st[0] += 1
                        return R[n % 2]

                    def transposes(which, tiles):
                        r = stage_wait()
                        if which == 0 and tiles[0] == 0:
                            pe.wait_ge(rope_ready, f + 1)
                        hold(pe)
                        for n, (w, t) in enumerate([(which, t) for t in tiles] if tiles[0] < 8 else [(0, 8), (1, 8)]):
                            mm = pe.transpose(r[0:DK, n * P:(n + 1) * P], qkr[:, t, w, :], ident[:, :])
                        mm.then_inc(st_ready, 1)

                    def kv(c0_):
                        r = stage_wait()
                        pe.wait_ge(kz_ready, f + 1)
                        for n in range(4):
                            mm = pe.matmul(r[0:DK, n * P:(n + 1) * P], kz[:, c0_ + n, :], tok[:, c0_ + n, P:2 * P], start=True, stop=True)
                        mm.then_inc(st_ready, 1)

                    def score(c0_):
                        r = stage_wait()
                        pe.wait_ge(qkT_ready, f + 1)
                        for n in range(4):
                            c = slice((c0_ + n) * P, (c0_ + n + 1) * P)
                            mm = pe.matmul(r[:, n * P:(n + 1) * P], kT[:, c], qT[:, c], start=True, stop=True)
                        mm.then_inc(st_ready, 1)

                    def score_s():
                        r = stage_wait()
                        pe.wait_ge(qkT_ready, f + 1)
                        hold(pe)
                        mm = pe.matmul(r[0:TS, 0:TS], kT[:, SEQ:T], qT[:, SEQ:T], start=True, stop=True)
                        mm.then_inc(st_ready, 1)

                    def kv_s(b0):
                        r = stage_wait()
                        pe.wait_ge(kz_ready, f + 1)
                        hold(pe)
                        for n in range(4):
                            mm = pe.matmul(r[0:DK, n * P:(n + 1) * P], kzb[:, b0 + n, :], tok[0:TS, NT - 1, P:2 * P], start=True, stop=True)
                        mm.then_inc(st_ready, 1)

                    def outp(c0_):
                        r = stage_wait()
                        if c0_ == 0:
                            pe.wait_ge(pT_ready, f + 1)
                        for n in range(4):
                            c = c0_ + n
                            mm = pe.matmul(r[:, n * P:(n + 1) * P], tok[:, c, P:2 * P], pT[:, c, :], start=True, stop=(c == 0))
                            if c:
                                mm = pe.matmul(r[:, n * P:(n + 1) * P], Sall[:, c, :], qxi[:, c * P:(c + 1) * P], start=False, stop=True)
                        mm.then_inc(st_ready, 1)

                    def outp_s():
                        r = stage_wait()
                        pe.wait_ge(S0_in, f * 16 + 16)
                        pe.matmul(r[:, 0:TS], tok[0:TS, NT - 1, P:2 * P], pTs[:, :], start=True, stop=False)
                        for b in range(NB):
                            mm = pe.matmul(r[:, b * NS:(b + 1) * NS], S0[:, b, :], qxi[:, SEQ + b * NS:SEQ + (b + 1) * NS], start=False, stop=(b == NB - 1))
                        mm.then_inc(st_ready, 1)

                    def spread(s, src, wait):
                        a, e = SLICES[s]
                        r = stage_wait()
                        pe.wait_ge(*wait)
                        dst = r[:, 0:e - a]
                        mm = pe.matmul(dst, onesm[:, :], src[:, a:e], start=True, stop=True)
                        mm.then_inc(st_ready, 1)

                    for s in range(3):
                        part(1, "pj", s, pj_ready, f * 5 + 2)
                    part(2, "pk", 0, pk_ready, f * 4 + 2)
                    transposes(0, range(0, 4))
                    transposes(0, range(4, 8))
                    part(2, "pk", 1, pk_ready, f * 4 + 2)
                    part(2, "pk", 2, pk_ready, f * 4 + 2)
                    transposes(1, range(0, 4))
                    transposes(1, range(4, 8))
                    part(3, "pj", 0, pj_ready, f * 5 + 3)
                    transposes(0, (8,))
                    kv(0)
                    part(3, "pj", 1, pj_ready, f * 5 + 3)
                    part(3, "pj", 2, pj_ready, f * 5 + 3)
                    kv(4)
                    score(0)
                    part(4, "pk", 0, pk_ready, f * 4 + 3)
                    score(4)
                    score_s()
                    part(4, "pk", 1, pk_ready, f * 4 + 3)
                    part(4, "pk", 2, pk_ready, f * 4 + 3)
                    kv_s(0)
                    kv_s(4)
                    pe.wait_ge(xl_ready, f + 1)
                    pe.wait_ge(wab_in, f * 32 + 32)
                    lru_gate(0, "pj", pj_ready)
                    part(5, "pk", 0, pk_ready, f * 4 + 4)
                    outp(0)
                    outp(4)
                    part(5, "pk", 1, pk_ready, f * 4 + 4)
                    part(5, "pk", 2, pk_ready, f * 4 + 4)
                    outp_s()
                    lru_gate(1, "pj", pj_ready)
                    pe.wait_ge(pj_ready, f * 5 + 5)
                    pe.sem_inc(wab_used, 1)
                    if not last:
                        qkv_high(f + 1)
                    for s in range(3):
                        spread(s, osb, (o_ready, f + 1))
                    if not last:
                        qkv_low(f + 1)
                    for s in range(3):
                        spread(s, dsq, (dsq_ready, f + 1))
                    assert st[0] == NST + NVAR
                qkv_high(0)
                qkv_low(0)
                with pe.Fori(0, H - 1) as f:
                    head(f, False)
                head(H - 1, True)

            @block.vector
            def _(v):
                v.sem_inc(xr_used, 1)
                v.sem_inc(f_done, 1)
                v.sem_inc(st_out, 32)
                v.sem_inc(mg_out, 16)
                v.memset(xr[:, 0:HIST], 0.0)
                v.memset(las[:, :, 0:1], 0.0)
                v.wait_ge(tab_in, 160)
                with v.Fori(0, H) as f:
                    fs = bass.ds(f, 1)
                    dl_.loop(f, 23)
                    st = [0]

                    def stage():
                        st[0] += 1
                        v.wait_ge(st_ready, f * (NST + NVAR) + st[0])
                        return R[(st[0] - 1) % 2]
                    v.wait_ge(qkv_ready, f + 1)
                    qk = tok[:, :, 0:2 * DK].rearrange("p t (w d) -> p t w d", w=2)
                    sh = [P, NT, 2, DK]
                    v.tensor_tensor(qkr[:, :, :, :], qk, bc(rope_c[:, :, :], 2, sh), ALU.mult)
                    hf = DK // 2
                    sh = [P, NT, 2, hf]
                    v.tensor_tensor(rt[:, :, :, 0:hf], qk[:, :, :, hf:], bc(rope_s[:, :, 0:hf], 2, sh), ALU.mult)
                    dl_(v.tensor_tensor(rt[:, :, :, hf:], qk[:, :, :, 0:hf], bc(rope_s[:, :, hf:], 2, sh), ALU.mult))
                    v.tensor_tensor(qkr[:, :, :, :], qkr[:, :, :, :], rt[:, :, :, :], ALU.add).then_inc(rope_ready, 1)
                    v.wait_ge(rope_ready, f + 1)
                    v.tensor_scalar(kz[:, :, :], qkr[:, 0:NT - 1, 1, :], zeta[:, fs], None, ALU.mult)
                    v.tensor_tensor(kzb[:, :, :], bc(qkr[0:TS, NT - 1, 1, :], 1, [TS, NB, DK]),
                                    szeta[:, fs, :].rearrange("p o b -> p (o b)").unsqueeze(2).broadcast_to([TS, NB, DK]), ALU.mult).then_inc(kz_ready, 1)
                    v.wait_ge(xr_ready, f + 1)
                    xls = seqs(xl[:, SEQ:T], NS)
                    v.tensor_scalar(xl[:, 0:SEQ], xr[:, 0:SEQ], vec[:, V_CW, fs], vec[:, V_CB, fs], ALU.mult, ALU.add)
                    dl_(v.tensor_scalar(xls, xrs[:, :, 0:NS], vec[:, V_CW, fs], vec[:, V_CB, fs], ALU.mult, ALU.add))
                    for j in range(1, CONV):
                        v.scalar_tensor_tensor(xl[:, 0:SEQ], xr[:, j:j + SEQ], vec[:, V_CW + j, fs], xl[:, 0:SEQ], ALU.mult, ALU.add)
                        ins = v.scalar_tensor_tensor(xls, xrs[:, :, j:j + NS], vec[:, V_CW + j, fs], xls, ALU.mult, ALU.add)
                        if j < CONV - 1:
                            dl_(ins)
                        else:
                            ins.then_inc(xl_ready, 1)
                    v.tensor_copy(convo[:, fs, 0:HIST], xr[:, SEQ:XR].unsqueeze(1))
                    v.tensor_copy(convo[:, fs, HIST:].rearrange("p o (b j) -> p (o b) j", j=HIST), xrs[:, :, NS:]).then_inc(xr_used, 1)
                    for n in range(2):
                        r = stage()
                        v.tensor_copy(qT[:, n * 512:(n + 1) * 512], r[0:DK, :]).then_inc(st_free, 1)
                    for n in range(2):
                        r = stage()
                        v.tensor_scalar(kT[:, n * 512:(n + 1) * 512], r[0:DK, :], DK ** -0.5, None, ALU.mult).then_inc(st_free, 1)
                    r = stage()
                    dl_(v.tensor_copy(qT[:, SEQ:TPAD], r[0:DK, 0:P]))
                    v.tensor_scalar(kT[:, SEQ:TPAD], r[0:DK, P:2 * P], DK ** -0.5, None, ALU.mult).then_inc(qkT_ready, 1)
                    v.wait_ge(qkT_ready, f + 1)
                    v.sem_inc(st_free, 1)
                    v.tensor_tensor(seqs(qxi[:, 0:SEQ], P), seqs(qT[:, 0:SEQ], P), xi[:, fs, :].broadcast_to([DK, NT - 1, P]), ALU.mult)
                    dl_(v.tensor_tensor(seqs(qxi[:, SEQ:T], NS), seqs(qT[:, SEQ:T], NS), xi[:, fs, 0:NS].broadcast_to([DK, NB, NS]), ALU.mult))
                    v.wait_ge(st_out, f * 32 + 32)
                    for q in range(2):
                        r = stage()
                        for n in range(4):
                            c = 4 * q + n
                            kvp = r[0:DK, n * P:(n + 1) * P]
                            if c == 0:
                                ins = v.tensor_copy(Sall[:, 1, :], kvp)
                            else:
                                ins = v.scalar_tensor_tensor(Sall[:, c + 1, :], Sall[:, c, :], gch[:, 0, fs], kvp, ALU.mult, ALU.add)
                            if c < 7:
                                dl_(ins)
                            else:
                                ins.then_inc(S_ready, 1)
                                v.wait_ge(S_ready, f + 1)
                        v.sem_inc(st_free, 1)
                    for q in range(2):
                        r = stage()
                        v.tensor_tensor(pT[:, 4 * q:4 * q + 4, :], seqs(r[:, :], P), dmask[:, fs, :].broadcast_to([P, 4, P]), ALU.mult).then_inc(st_free, 1)
                    r = stage()
                    v.tensor_tensor(pTs[:, :], r[0:TS, 0:TS], smask[:, fs, :].rearrange("p o m -> p (o m)"), ALU.mult).then_inc(pT_ready, 1)
                    v.wait_ge(pT_ready, f + 1)
                    v.sem_inc(st_free, 1)
                    v.wait_ge(S0_in, f * 16 + 16)
                    for q in range(2):
                        r = stage()
                        v.scalar_tensor_tensor(Sout[:, 4 * q:4 * q + 4, :], S0[:, 4 * q:4 * q + 4, :], gch[:, 1, fs], seqs(r[0:DK, :], P), ALU.mult, ALU.add).then_inc(Sout_ready, 1)
                        v.wait_ge(Sout_ready, f * 2 + q + 1)
                        v.sem_inc(st_free, 1)
                    v.wait_ge(gret_ready, f + 1)
                    v.wait_ge(ga_ready, f + 1)
                    v.tensor_tensor(gret[:, :], gret[:, :], gate[:, :], ALU.mult).then_inc(ga_used, 1)
                    v.wait_ge(mg_out, f * 16 + 16)
                    for q in range(2):
                        r = stage()
                        v.tensor_copy(osb[:, q * 512:(q + 1) * 512], r[:, :]).then_inc(st_free, 1)
                    r = stage()
                    v.tensor_copy(osb[:, SEQ:T], r[:, 0:TS]).then_inc(o_ready, 1)
                    v.wait_ge(o_ready, f + 1)
                    v.sem_inc(st_free, 1)
                    v.sem_inc(S0_used, 1)
                    v.wait_ge(th_ready, f + 1)
                    dl_(v.tensor_scalar(om[:, :], th[:, :], -1.0, 1.0, ALU.mult, ALU.add))
                    dl_(v.reciprocal(om[:, :], om[:, :]))
                    v.scalar_tensor_tensor(om[:, :], th[:, :], -2.0, om[:, :], ALU.mult, ALU.mult).then_inc(m2_ready, 1)
                    v.wait_ge(i_ready, f + 1)
                    dl_(v.tensor_tensor(ig[:, :], ig[:, :], xl[:, :], ALU.mult))
                    for n, (a, b) in enumerate(SLICES):
                        r = stage()
                        src = r[:, 0:b - a]
                        ins = v.tensor_tensor(osb[:, a:b], osb[:, a:b], src, ALU.subtract)
                        ins.then_inc(st_free if n < 2 else d_ready, 1)
                    v.wait_ge(d_ready, f + 1)
                    v.sem_inc(st_free, 1)
                    assert st[0] == NST
                    v.wait_ge(mult_ready, f + 1)
                    v.wait_ge(a_ready, f + 1)
                    v.tensor_copy(lbs[:, :, 0:1], h0[:, fs, :].rearrange("p o b -> p (o b)").unsqueeze(2))
                    v.tensor_tensor(lb[:, 0:SEQ], ig[:, 0:SEQ], om[:, 0:SEQ], ALU.mult)
                    dl_(v.tensor_tensor(lbs[:, :, 1:], seqs(ig[:, SEQ:T], NS), seqs(om[:, SEQ:T], NS), ALU.mult))
                    dl_(v.tensor_tensor_scan(lh[:, :], la[:, :], lb[:, :], 0.0, ALU.mult, ALU.add))
                    v.tensor_copy(lruo[:, fs, 0:1], lh[:, SEQ - 1:SEQ].unsqueeze(1))
                    v.tensor_copy(lruo[:, fs, 1:], lhs_[:, :, NS].unsqueeze(1))
                    v.wait_ge(glru_ready, f + 1)
                    v.tensor_tensor(glru[:, 0:SEQ], glru[:, 0:SEQ], lh[:, 0:SEQ], ALU.mult)
                    dl_(v.tensor_tensor(seqs(glru[:, SEQ:T], NS), seqs(glru[:, SEQ:T], NS), lhs_[:, :, 1:], ALU.mult))
                    v.wait_ge(gb_ready, f + 1)
                    dl_(v.tensor_tensor(glru[:, :], glru[:, :], gate[:, :], ALU.mult))
                    v.wait_ge(sdv_ready, f * 3 + 3)
                    dl_(v.reciprocal(dsq[:, :], dsq[:, :]))
                    dl_(v.scalar_tensor_tensor(osb[:, :], osb[:, :], vec[:, V_GN, fs], dsq[:, :], ALU.mult, ALU.mult))
                    dl_(v.tensor_tensor(osb[:, :], osb[:, :], gret[:, :], ALU.mult))
                    v.tensor_tensor(osb[:, :], osb[:, :], glru[:, :], ALU.add).then_inc(mg_ready, 1)
                    v.wait_ge(mg_ready, f + 1)
                    v.sem_inc(f_done, 1)
                dl_.end(H)
        for ch in (al_, gl_):
            ch.flat()
        s1.close()

        late = ExitStack()
        hn2T = sb(late, "hn2T", [P, KC, T])
        s2 = ExitStack()
        mgT, x2T = sb(s2, "mgT", [P, KC, T]), sb(s2, "x2T", [P, KC, T])
        sq2 = [sb(s2, f"sqb{u}", [P, T]) for u in range(2)]
        rstd2, gain2, tmp2 = sb(s2, "rstd2", [P, T]), sb(s2, "gain2", [P, KC, 1 + NB]), sb(s2, "tmp2", [P, KC, TS])
        mgi, x2_in, x2_out = sem("mgi"), sem("x2_in"), sem("x2_out")
        o2_ready, o2_free, x2_ready, sq2_ready, ssum2, sd2 = (sem(n) for n in ("o2_ready", "o2_free", "x2_ready", "sq2_ready", "ssum2", "sd2"))

        with nc.Block() as block:
            @block.sync
            def _(sp):
                sp.dma_start(mgT[:, :, :], S["mg"].rearrange("f p t -> p f t")).then_inc(mgi, 16)
                sp.dma_start(x2T[:, :, :], I["xT"].rearrange("(k p) t -> p k t", p=P)).then_inc(x2_in, 16)
                sp.wait_ge(x2_ready, KC)
                sp.dma_start(S["x2"].rearrange("k p t -> p k t"), x2T[:, :, :]).then_inc(x2_out, 16)
                sp.wait_ge(x2_out, 16)

            @block.tensor
            def _(pe):
                pe.wait_ge(wo_in, 16)
                pe.wait_ge(mgi, 16)
                for m in range(KC):
                    acc = pj if m % 2 == 0 else pk
                    if m >= 2:
                        pe.wait_ge(o2_free, m - 1)
                    for a, e in SLICES:
                        for k in range(KC):
                            mm = pe.matmul(acc[:, a:e], wo[:, k, m * P:(m + 1) * P], mgT[:, k, a:e], start=(k == 0), stop=(k == KC - 1))
                    mm.then_inc(o2_ready, 1)
                pe.wait_ge(o2_free, KC)
                for k in range(KC):
                    pe.wait_ge(sq2_ready, k + 1)
                    for a, e in SLICES:
                        mm = pe.matmul(pj[:, a:e], ones[:, :], sq2[k % 2][:, a:e], start=(k == 0), stop=(k == KC - 1))
                    mm.then_inc(ssum2, 1)

            @block.scalar
            def _(act):
                for k in range(KC):
                    act.wait_ge(x2_ready, k + 1)
                    if k >= 2:
                        act.wait_ge(ssum2, k - 1)
                    act.activation(sq2[k % 2][:, :], x2T[:, k, :], ACT.Square).then_inc(sq2_ready, 1)
                act.wait_ge(ssum2, KC)
                act.activation(rstd2[:, :], pj[:, 0:T], ACT.Sqrt, bias=epsb[:, 0:1], scale=1.0 / D).then_inc(sd2, 1)
                add_shift(hn2T, modT[:, SH2:SH2 + 8, :], KC)

            @block.vector
            def _(v):
                v.wait_ge(x2_in, 16)
                for m in range(KC):
                    acc = pj if m % 2 == 0 else pk
                    v.wait_ge(o2_ready, m + 1)
                    v.scalar_tensor_tensor(x2T[:, m, 0:SEQ], acc[:, 0:SEQ], modT[:, G1 + m, 0:1], x2T[:, m, 0:SEQ], ALU.mult, ALU.add)
                    dl_(v.tensor_tensor(seqs(tmp2[:, m, :], NS), seqs(acc[:, SEQ:T], NS), bc(modT[:, G1 + m, 1:1 + NB], 2, [P, NB, NS]), ALU.mult))
                    v.tensor_tensor(x2T[:, m, SEQ:T], x2T[:, m, SEQ:T], tmp2[:, m, :], ALU.add).then_inc(x2_ready, 1)
                    v.sem_inc(o2_free, 1)
                dl_(v.scalar_tensor_tensor(gain2[:, :, :], modT[:, SC2:SC2 + 8, :], 1.0, bc(vec[:, V_N2, :], 2, [P, KC, 9]), ALU.add, ALU.mult))
                v.wait_ge(sd2, 1)
                dl_(v.reciprocal(rstd2[:, :], rstd2[:, :]))
                adjust(dl_, x2T, hn2T, rstd2, gain2, modT[:, SH2:SH2 + 8, :], tmp2)
        dl_.flat()
        s2.close()

        s3 = ExitStack()
        wq = [sb(s3, f"wq{u}", [P, KC, P]) for u in range(2)]
        keys = sb(s3, "keys", [P, 2, NKEY])
        stg = [sb(s3, f"stg{u}", [P, D]) for u in range(2)]
        qh = [sb(s3, f"qh{u}", [P, T]) for u in range(2)]
        sc = [sb(s3, f"sc{u}", [P, NT, NKEY]) for u in range(2)]
        tv = [sb(s3, f"tv{u}", [P, NT, TOPK]) for u in range(2)]
        ti = [sb(s3, f"ti{u}", [P, NT, TOPK], U32) for u in range(2)]
        tf = [sb(s3, f"tf{u}", [P, NT, TOPK]) for u in range(2)]
        cand, cid = sb(s3, "cand", [P, NT, NCAND]), sb(s3, "cid", [P, NT, NCAND])
        bv = sb(s3, "bv", [P, NT, TOPK])
        bp, bpf = sb(s3, "bp", [P, NT, TOPK], U32), sb(s3, "bpf", [P, NT, TOPK])
        hot = sb(s3, "hot", [P, NT, TOPK, NCAND])
        eidf = sb(s3, "eidf", [P, NT, H + 1, TOPK])
        gsum = sb(s3, "gsum", [P, NT * H])
        wq_in, wq_used = [sem("wq_in0"), sem("wq_in1")], sem("wq_used")
        key_in, q_ps, qh_ready, s_ps, s_ready, s_used, z_ready = (sem(n) for n in ("key_in", "q_ps", "qh_ready", "s_ps", "s_ready", "s_used", "z_ready"))
        tr_ready, tr_free, stg_ready = (sem(n) for n in ("tr_ready", "tr_free", "stg_ready"))
        stg_out = [sem("stg_out0"), sem("stg_out1")]
        pos_ready, hot_ready, exp_ready, max_ready = (sem(n) for n in ("pos_ready", "hot_ready", "exp_ready", "max_ready"))

        with nc.Block() as block:
            @block.sync
            def _(sp):
                sp.dma_start(keys[:, :, :], I["keys"]).then_inc(key_in, 16)
                sp.dma_start(iota[:, :], I["iota"]).then_inc(key_in, 16)

                def load(h, u):
                    src = I["peer_wq"][:, bass.ds(h * 256 + u * P, P)].rearrange("(k p) n -> p k n", p=P)
                    sp.dma_start(wq[u][:, :, :], src).then_inc(wq_in[u], 16)
                load(0, 0)
                load(0, 1)
                with sp.Fori(1, H) as h:
                    for u in range(2):
                        sp.wait_ge(wq_used, h * 2 + (u - 1))
                        load(h, u)
                for t in range(NT):
                    sp.wait_ge(stg_ready, t + 1)
                    sp.dma_start(S["hn2"][t], stg[t % 2][:, :]).then_inc(stg_out[t % 2], 16)
                sp.wait_ge(stg_out[0], 16 * ((NT + 1) // 2))
                sp.wait_ge(stg_out[1], 16 * (NT // 2))

            @block.tensor
            def _(pe):
                pe.wait_ge(key_in, 32)
                with pe.Fori(0, H) as h:
                    for u in range(2):
                        acc = (pj, pk)[u]
                        pe.wait_ge(wq_in[u], h * 16 + 16)
                        pe.wait_ge(s_ready, h * 2 + (u + 1))
                        for a, e in SLICES:
                            for k in range(KC):
                                mm = pe.matmul(acc[:, a:e], wq[u][:, k, :], hn2T[:, k, a:e], start=(k == 0), stop=(k == KC - 1))
                        mm.then_inc(q_ps, 1)
                        pe.wait_ge(q_ps, h * 2 + (u + 1))
                        pe.sem_inc(wq_used, 1)
                    for u in range(2):
                        acc = (pj, pk)[u]
                        pe.wait_ge(qh_ready, h * 2 + (u + 1))
                        for t in range(NT):
                            c = slice(t * P, min((t + 1) * P, T))
                            mm = pe.matmul(acc[0:c.stop - c.start, t * NKEY:(t + 1) * NKEY], qh[u][:, c], keys[:, u, :], start=True, stop=True)
                        mm.then_inc(s_ps, 1)
                n = 0
                for t in range(NT):
                    c = slice(t * P, min((t + 1) * P, T))
                    w = c.stop - c.start
                    for q in range(2):
                        if n >= 2:
                            pe.wait_ge(tr_free, n - 1)
                        for j in range(4):
                            mm = pe.transpose(R[q][0:w, j * P:(j + 1) * P], hn2T[:, 4 * q + j, c], ident[:, :])
                        mm.then_inc(tr_ready, 1)
                        n += 1

            @block.scalar
            def _(act):
                act.sem_inc(s_ready, 2)
                act.wait_ge(z_ready, 2)
                with act.Fori(0, H) as h:
                    for u in range(2):
                        act.wait_ge(q_ps, h * 2 + (u + 1))
                        act.activation(qh[u][:, :], (pj, pk)[u][:, 0:T], ACT.Copy).then_inc(qh_ready, 1)
                    for u in range(2):
                        acc = (pj, pk)[u]
                        act.wait_ge(s_ps, h * 2 + (u + 1))
                        act.wait_ge(s_used, h * 2 + (u + 1))
                        act.activation(sc[u][:, 0:8, :], acc[:, 0:SEQ].rearrange("p (t n) -> p t n", n=NKEY), ACT.Copy)
                        act.activation(sc[u][0:TS, 8, :], acc[0:TS, SEQ:SEQ + NKEY], ACT.Copy).then_inc(s_ready, 1)
                n = 0
                for t in range(NT):
                    w = P if t < NT - 1 else TS
                    if t >= 2:
                        act.wait_ge(stg_out[t % 2], 16 * (t // 2))
                    for q in range(2):
                        act.wait_ge(tr_ready, n + 1)
                        act.activation(stg[t % 2][0:w, q * 512:(q + 1) * 512], R[q][0:w, :], ACT.Copy).then_inc(tr_free, 1)
                        n += 1
                    act.wait_ge(tr_free, n)
                    act.sem_inc(stg_ready, 1)
                act.wait_ge(max_ready, 1)
                act.activation(gw[:, :, :, :], gw[:, :, :, :], ACT.Exp).then_inc(exp_ready, 1)

            @block.gpsimd
            def _(g):
                g.wait_ge(key_in, 32)
                g.memset(hot[:, :, :, :], 0.0).then_inc(hot_ready, 1)

                def products(h, link, tiles):
                    g.wait_ge(pos_ready, h + 1)
                    n = tiles.stop - tiles.start
                    link(g.tensor_tensor(hot[:, tiles, :, :], hot[:, tiles, :, :], bc(cid[:, tiles, :], 2, [P, n, TOPK, NCAND]), ALU.mult))
                    half = NCAND // 2
                    link(g.tensor_tensor(hot[:, tiles, :, 0:half], hot[:, tiles, :, 0:half], hot[:, tiles, :, half:], ALU.add))
                    g.tensor_tensor(hot[:, tiles, :, 0:half - SUMW], hot[:, tiles, :, 0:half - SUMW], hot[:, tiles, :, SUMW:half], ALU.add).then_inc(hot_ready, 1)
                with g.Fori(0, H - 1) as h:
                    gl_.loop(h, 2)
                    products(h, gl_, slice(0, NT))
                gl_.end(H - 1)
                products(H - 1, gl_, slice(0, TPOOL))

            @block.vector
            def _(v):
                v.sem_inc(s_used, 2)
                for u in range(2):
                    v.memset(sc[u][64:128, 8, :], 0.0).then_inc(z_ready, 1)
                v.tensor_copy(g2T[:, :, :], modT[:, G2:G2 + KC, :])
                v.tensor_copy(fnw[:, :], vec[:, V_FN, :])
                v.wait_ge(key_in, 32)

                def top16(src, vals, idxs):
                    hold(v)
                    for t in range(NT):
                        ins = v.max(vals[:, t, 0:8], src[:, t, :])
                    dl_(ins)
                    hold(v)
                    for t in range(NT):
                        v.max_index(idxs[:, t, 0:8], vals[:, t, 0:8], src[:, t, :])
                    for t in range(NT):
                        ins = v.match_replace(src[:, t, :], vals[:, t, 0:8], src[:, t, :], LOW)
                    dl_(ins)
                    hold(v)
                    for t in range(NT):
                        ins = v.max(vals[:, t, 8:16], src[:, t, :])
                    dl_(ins)
                    hold(v)
                    for t in range(NT):
                        ins = v.max_index(idxs[:, t, 8:16], vals[:, t, 8:16], src[:, t, :])
                    dl_(ins)

                def chosen(h, hs, tiles=slice(0, NT)):
                    v.wait_ge(hot_ready, h + 1)
                    out = eidf[:, tiles, hs, :].rearrange("p t o k -> p t (o k)")
                    dl_(v.tensor_reduce(out, hot[:, tiles, :, 0:SUMW], AX, ALU.add))

                with v.Fori(0, H) as h:
                    hs = bass.ds(h, 1)
                    dl_.loop(h, 18)
                    for u in range(2):
                        v.wait_ge(s_ready, h * 2 + (u + 3))
                        top16(sc[u], tv[u], ti[u])
                        v.sem_inc(s_used, 1)
                        dl_(v.tensor_scalar(tf[u][:, :, :], ti[u][:, :, :], float(NKEY) if u == 0 else 1.0, None, ALU.mult))

                    def pairs(out, x):
                        for i0, ni, nj, p0 in STAIRS:
                            shp = [P, NT, ni, nj]
                            ins = v.tensor_tensor(out[:, :, p0:p0 + ni * nj].rearrange("p t (i j) -> p t i j", j=nj),
                                                  bc(x[0][:, :, i0:i0 + ni], 3, shp), bc(x[1][:, :, 0:nj], 2, shp), ALU.add)
                        dl_(ins)
                    pairs(cand, tv)
                    top16(cand, bv, bp)
                    v.tensor_copy(gw[:, :, hs, :].rearrange("p t o k -> p t (o k)"), bv[:, :, :])
                    dl_(v.tensor_copy(bpf[:, :, :], bp[:, :, :]))
                    chosen(h, hs)
                    pairs(cid, tf)
                    shp = [P, NT, TOPK, NCAND]
                    v.tensor_tensor(hot[:, :, :, :], iota[:, 0:NCAND].unsqueeze(1).unsqueeze(1).broadcast_to(shp), bc(bpf[:, :, :], 3, shp), ALU.is_equal).then_inc(pos_ready, 1)
                dl_.end(H)
                gv = gw[:, :, :, :].rearrange("p t h k -> p (t h) k")
                dl_(v.tensor_copy(gsum[:, :], gv[:, :, 0]))
                v.tensor_tensor(gv, gv, bc(gsum[:, :], 2, [P, NT * H, TOPK]), ALU.subtract).then_inc(max_ready, 1)
                v.wait_ge(pos_ready, H)
                own = slice(TPOOL, NT)
                dl_(v.tensor_tensor(hot[:, own, :, :], hot[:, own, :, :], bc(cid[:, own, :], 2, [P, NT - TPOOL, TOPK, NCAND]), ALU.mult))
                v.tensor_reduce(eidf[:, own, H, :], hot[:, own, :, :], AX, ALU.add)
                v.wait_ge(max_ready, 1)
                v.wait_ge(exp_ready, 1)
                dl_(v.tensor_reduce(gsum[:, :], gv, AX, ALU.add))
                dl_(v.reciprocal(gsum[:, :], gsum[:, :]))
                dl_(v.tensor_tensor(gv, gv, bc(gsum[:, :], 2, [P, NT * H, TOPK]), ALU.mult))
                chosen(H, slice(H, H + 1), slice(0, TPOOL))
                v.tensor_copy(eidx[:, :, :].rearrange("p t (h k) -> p t h k", k=TOPK), eidf[:, :, 1:, :])
        dl_.flat()
        gl_.flat()
        s3.close()
        late.close()
        mix.close()
        mods.close()
        early.close()

        GT = 2 * P
        NGRP = SEQ // GT
        HK = NKEY // 2
        VB = 4
        SB = 4
        QB = P // SB
        VD = 4
        DU = 8
        W = sb(ctx, "W", [P, NKEY, GT])
        rows = sb(ctx, "rows", [P, VD, D])
        slots = sb(ctx, "slots", [P, 2, 8], U32)
        vbuf = sb(ctx, "vbuf", [P, VB, D])
        htok = [sb(ctx, f"htok{u}", [P, D]) for u in range(2)]
        oh2 = sb(ctx, "oh2", [P, 2, SB, NKEY], BF16)
        oh1 = sb(ctx, "oh1", [P, 2, SB, HK], BF16)
        oh1w = sb(ctx, "oh1w", [P, 2, 3, SB, HK], BF16)
        dist = sb(ctx, "dist", [P, SB, NKEY], BF16)
        acc = W[:, 0:KC // 2, :].rearrange("p e t -> p (e t)")
        e1s, e2s = sb(ctx, "e1s", [P, GT], BF16), sb(ctx, "e2s", [P, GT])
        wpart = sb(ctx, "wpart", [P, 3, GT], BF16)
        x3 = sb(ctx, "x3", [P, KC, GT])
        ev = sb(ctx, "ev", [P, KC, GT])
        rs4 = sb(ctx, "rs4", [P, GT])
        ef = sb(ctx, "ef", [P, 2, P])
        dots8, dots = sb(ctx, "dots8", [P, DU]), sb(ctx, "dots", [P, P])
        vacc = ctx.enter_context(nc.psum_tensor("vacc", [P, KC, GT], F32))
        scat = [ctx.enter_context(nc.psum_tensor(f"scat{i}", [P, 512], F32)) for i in range(2)]
        tps = ctx.enter_context(nc.psum_tensor("tps", [P, 512], F32))
        nps = ctx.enter_context(nc.psum_tensor("nps", [P, 512], F32))

        landed = [sem(f"landed{i}") for i in range(VD)]
        h_in, v_in = [sem("h_in0"), sem("h_in1")], [sem(f"v_in{i}") for i in range(VB)]
        (used, h_used, v_used, gelu_ready, dots_ready, slot_ready, tr4_ready, picks_ready, oh_ready, sc_ps, w_evac,
         vacc_ready, ev_ready, x2g_in, x3_ready, sq4_ready, n_ready, rs_ready, y_ready, y_out, ef_ready, acc_ready, oh2_ready, abs_ready, eq_ready) = (sem("s4_" + n) for n in (
            "used", "h_used", "v_used", "gelu_ready", "dots_ready", "slot_ready", "tr4_ready", "picks_ready", "oh_ready", "sc_ps", "w_evac",
            "vacc_ready", "ev_ready", "x2g_in", "x3_ready", "sq4_ready", "n_ready", "rs_ready", "y_ready", "y_out", "ef_ready", "acc_ready", "oh2_ready", "abs_ready", "eq_ready"))
        NG = P // 8

        def batch0(g, q):
            return g * (4 * QB) + (q + 2) * QB

        with nc.Block() as block:
            @block.sync
            def _(sp):
                def h_load(t, u):
                    sp.dma_start(htok[u][:, :], S["hn2"][bass.ds(t, 1)].rearrange("o p d -> p (o d)")).then_inc(h_in[u], 16)

                def v_stream(g, lo, hi):
                    with sp.Fori(lo, hi) as i:
                        for s in range(VB):
                            sp.wait_ge(v_used, g * NKEY + i * VB + (s + 1))
                            sp.dma_start(vbuf[:, s, :], I["peer_v"][bass.ds((i * VB + s) * P, P), :]).then_inc(v_in[s], 16)

                def x_load(g):
                    sp.dma_start(x3[:, :, :], S["x2"][:, :, bass.ds(g * GT, GT)].rearrange("k p t -> p k t")).then_inc(x2g_in, 16)

                def y_store(g):
                    sp.wait_ge(y_ready, g + 1)
                    sp.dma_start(O["y"][:, :, bass.ds(g * GT, GT)].rearrange("k p t -> p k t"), x3[:, :, :]).then_inc(y_out, 16)
                    sp.wait_ge(y_out, g * 16 + 16)
                cut = 5 * NKEY // VB // 8
                h_load(0, 0)
                h_load(1, 1)
                x_load(0)
                sp.wait_ge(h_used, 1)
                h_load(2, 0)
                sp.wait_ge(h_used, 2)
                h_load(3, 1)
                v_stream(0, 0, cut)
                sp.wait_ge(h_used, 3)
                h_load(4, 0)
                v_stream(0, cut, NKEY // VB)
                with sp.Fori(1, NGRP - 1) as g:
                    sp.wait_ge(h_used, g * 2 + 2)
                    h_load(g * 2 + 3, 1)
                    v_stream(g, 0, cut)
                    sp.wait_ge(h_used, g * 2 + 3)
                    h_load(g * 2 + 4, 0)
                    y_store(g - 1)
                    x_load(g)
                    v_stream(g, cut, NKEY // VB)
                v_stream(NGRP - 1, 0, cut)
                y_store(NGRP - 2)
                x_load(NGRP - 1)
                v_stream(NGRP - 1, cut, NKEY // VB)
                y_store(NGRP - 1)
                sp.dma_start(x3[:, :, 0:TS], S["x2"][:, :, SEQ:T].rearrange("k p t -> p k t")).then_inc(x2g_in, 16)
                sp.wait_ge(y_ready, NGRP + 1)
                sp.dma_start(O["y"][:, :, SEQ:T].rearrange("k p t -> p k t"), x3[:, :, 0:TS]).then_inc(y_out, 16)
                sp.wait_ge(y_out, 16 * NGRP + 16)

            @block.gpsimd
            def _(g):
                def gathers(grp, h, col, t, table, n):
                    g.wait_ge(used, grp * 8)
                    hold(g)
                    g.tensor_copy(slots[0:n, h, :], eidx[0:n, bass.ds(t, 1), bass.ds(col, 8)].rearrange("p o c -> p (o c)")).then_inc(slot_ready, 1)
                    g.wait_ge(slot_ready, grp + 1)
                    for s in range(8):
                        g.wait_ge(used, grp * 8 + (s + 9 - VD))
                        hold(g)
                        g.indirect_dma_start(rows[0:n, s % VD, :], None, table[:, :], bass.IndirectOffsetOnAxis(ap=slots[0:n, h, s:s + 1], axis=0)).then_inc(landed[s % VD], 16)

                def table_rows(first, t, table, n):
                    with g.Fori(0, NG // 2) as i:
                        for h in range(2):
                            gathers(first + i * 2 + h, h, i * 16 + h * 8, t, table, n)
                with g.Fori(0, NT - 1) as t:
                    table_rows(t * NG, t, I["peer_u"], P)
                table_rows((NT - 1) * NG, NT - 1, I["peer_u"], TS)
                table_rows(NT * NG, NT - 1, I["peer_v"], TS)

            @block.vector
            def _(v):
                v.sem_inc(used, 8)

                def dot(t, u, c0, s):
                    v.wait_ge(landed[s % VD], t * (P * 4) + c0 * 4 + 16 * (s // VD + 1))
                    v.tensor_tensor_reduce(rows[:, s % VD, :], rows[:, s % VD, :], htok[u][:, :], 1.0, 0.0, ALU.mult, ALU.add, dots8[:, s:s + 1]).then_inc(used, 1)

                def dots_free(t, c):
                    v.wait_ge(dots_ready, t * (P // DU) + c + 1)

                def dots_keep(t, c0, c):
                    v.wait_ge(used, t * P + c0 + (DU + 8))
                    v.tensor_copy(dots[:, bass.ds(c0, DU)], dots8[:, :]).then_inc(dots_ready, 1)

                def dots_alone(t, u, lo, hi):
                    with v.Fori(lo, hi) as i:
                        dots_free(t, i)
                        for s in range(DU):
                            dot(t, u, i * DU, s)
                        dots_keep(t, i * DU, i)

                def tile_weights(t):
                    v.sem_inc(h_used, 1)
                    v.wait_ge(gelu_ready, t + 1)
                    return v.tensor_tensor(dots[:, :], dots[:, :], gw[:, bass.ds(t, 1), :, :].rearrange("p o h k -> p (o h k)"), ALU.mult)

                def tile_picks(t, u, link):
                    e = eidx[:, bass.ds(t, 1), :].rearrange("p o c -> p (o c)")
                    n = [ef[:, w, :].bitcast(U32) for w in range(2)]
                    v.tensor_scalar(n[0], e, 7, None, ALU.logical_shift_right)
                    link(v.tensor_scalar(n[1], e, NKEY - 1, None, ALU.bitwise_and))
                    for w in range(2):
                        v.tensor_copy(ef[:, w, :], n[w])
                    tile_weights(t).then_inc(ef_ready, 1)
                    v.wait_ge(tr4_ready, t + 1)
                    us = slice(u * P, (u + 1) * P)
                    v.tensor_copy(e1s[:, us], tps[:, P:2 * P])
                    v.tensor_copy(e2s[:, us], tps[:, 2 * P:3 * P])
                    link(v.tensor_copy(dots[:, :], tps[:, 0:P]))
                    for j in range(3):
                        ins = v.tensor_copy(wpart[:, j, us], dots[:, :])
                        if j < 2:
                            link(ins)
                            link(v.tensor_tensor(dots[:, :], dots[:, :], wpart[:, j, us], ALU.subtract))
                    ins.then_inc(picks_ready, 1)
                    v.wait_ge(picks_ready, t + 1)

                def quarter(b0, u, half, dots_of, lo=0, hi=P // 16):
                    t, tu, c0, nu = dots_of or (0, 0, 0, 0)
                    hold(v)
                    with v.Fori(lo, hi) as i:
                        for q in range(VB):
                            h = q % 2
                            v.wait_ge(sc_ps, b0 + i * VB + (q + 1))
                            k = bass.ds(i * (VB * SB) + (u * P + q * SB), SB)
                            v.tensor_tensor(oh1[:, h, :, :], bc(iota[:, half * HK:(half + 1) * HK], 1, [P, SB, HK]), bc(e1s[:, k], 2, [P, SB, HK]), ALU.is_equal).then_inc(eq_ready, 1)
                            v.wait_ge(eq_ready, b0 + i * VB + (q + 1))
                            v.tensor_tensor(oh1w[:, h, :, :, :], bc(oh1[:, h, :, :], 1, [P, 3, SB, HK]), bc(wpart[:, :, k], 3, [P, 3, SB, HK]), ALU.mult).then_inc(oh_ready, 1)
                            for m in range(q * nu * DU // VB, (q + 1) * nu * DU // VB):
                                c, s = i * nu + (c0 + m // DU), m % DU
                                if s == 0:
                                    dots_free(t, c)
                                dot(t, tu, c * DU, s)
                                if s == DU - 1:
                                    dots_keep(t, c * DU, c)

                def residual(g):
                    v.wait_ge(ev_ready, g + 2)
                    v.wait_ge(x2g_in, g * 16 + 16)
                    v.tensor_tensor(x3[:, :, :], x3[:, :, :], ev[:, :, :], ALU.add).then_inc(x3_ready, 1)

                def norm(g, link):
                    v.wait_ge(rs_ready, g + 1)
                    link(v.reciprocal(rs4[:, :], rs4[:, :]))
                    for k in range(KC):
                        ins = v.scalar_tensor_tensor(x3[:, k, :], x3[:, k, :], fnw[:, k:k + 1], rs4[:, :], ALU.mult, ALU.mult)
                    ins.then_inc(y_ready, 1)

                def group(g, first, last):
                    quarter(batch0(g, 0), 0, 1, (g * 2 + 2, 0, P // DU // 2, 1), 0, 2)
                    if not first:
                        residual(g - 1)
                    quarter(batch0(g, 0), 0, 1, (g * 2 + 2, 0, P // DU // 2, 1), 2, P // 16)
                    if last:
                        tile_weights(NT - 1).then_inc(ef_ready, 1)
                    else:
                        tile_picks(g * 2 + 2, 0, dl_)
                        v.wait_ge(h_in[1], g * 16 + 32)
                    quarter(batch0(g, 1), 1, 1, None if last else (g * 2 + 3, 1, 0, 1))
                    if not first:
                        norm(g - 1, dl_)
                    if not last:
                        quarter(batch0(g, 2), 0, 0, (g * 2 + 3, 1, P // DU // 2, 1))
                        tile_picks(g * 2 + 3, 1, dl_)
                        v.wait_ge(h_in[0], g * 16 + 48)
                        quarter(batch0(g, 3), 1, 0, (g * 2 + 4, 0, 0, 1))
                v.sem_inc(dots_ready, 1)
                v.sem_inc(sc_ps, 2)
                v.wait_ge(h_in[0], 16)
                dots_alone(0, 0, 0, P // DU)
                tile_picks(0, 0, dl_)
                v.wait_ge(h_in[1], 16)
                quarter(0, 0, 0, (1, 1, 0, 2))
                tile_picks(1, 1, dl_)
                v.wait_ge(h_in[0], 32)
                quarter(QB, 1, 0, (2, 0, 0, 1))
                group(0, True, False)
                with v.Fori(1, NGRP - 1) as g:
                    dl_.loop(g - 1, 13)
                    group(g, False, False)
                dl_.end(NGRP - 2)
                group(NGRP - 1, False, True)
                v.wait_ge(ef_ready, NT)
                v.wait_ge(v_used, NGRP * NKEY - NKEY // 2 + VB)
                dl_(v.memset(acc[0:TS, :], 0.0))
                r = slice(0, TS)
                hold(v)
                with v.Fori(0, P // 16) as i:
                    for s in range(16):
                        v.wait_ge(used, i * 16 + (NT * P + 8 + s))
                        v.wait_ge(landed[s % VD], i * 64 + (NT * P * 4 + 16 * (s // VD + 1)))
                        v.scalar_tensor_tensor(acc[r, :], rows[r, s % VD, :], dots[r, bass.ds(i * 16 + s, 1)], acc[r, :], ALU.mult, ALU.add).then_inc(used, 1)
                v.wait_ge(used, (NT + 1) * P + 8)
                v.sem_inc(acc_ready, 1)
                residual(NGRP - 1)
                norm(NGRP - 1, dl_)
                v.wait_ge(tr4_ready, NT)
                v.wait_ge(x2g_in, NGRP * 16 + 16)
                xs = x3[:, :, 0:TS]
                a4 = tps[:, :].rearrange("p (k b t) -> p k b t", k=KC, t=NS)
                p4 = ev[:, 0:2, :].rearrange("p w (k t) -> p (w k) t", t=TS)
                dl_(v.tensor_tensor(p4.rearrange("p k (b t) -> p k b t", t=NS), a4, bc(g2T[:, :, 1:1 + NB], 3, [P, KC, NB, NS]), ALU.mult))
                v.tensor_tensor(xs, xs, p4, ALU.add).then_inc(x3_ready, 1)
                v.wait_ge(rs_ready, NGRP + 1)
                dl_(v.reciprocal(rs4[:, 0:TS], rs4[:, 0:TS]))
                dl_(v.tensor_tensor(xs, xs, bc(rs4[:, 0:TS], 1, [P, KC, TS]), ALU.mult))
                v.tensor_tensor(xs, xs, bc(fnw[:, :], 2, [P, KC, TS]), ALU.mult).then_inc(y_ready, 1)
                dl_.flat()

            @block.scalar
            def _(act):
                act.sem_inc(w_evac, 2)
                act.sem_inc(ev_ready, 1)
                act.sem_inc(oh2_ready, 1)

                def gelu(t):
                    act.wait_ge(dots_ready, t * (P // DU) + (P // DU + 1))
                    act.activation(dots[:, :], dots[:, :], ACT.Gelu_apprx_tanh).then_inc(gelu_ready, 1)

                def hot(b0, u, i, q):
                    b, h = b0 + i * VB + q, q % 2
                    act.wait_ge(sc_ps, b + 1)
                    act.wait_ge(oh2_ready, b + 1)
                    for n in range(SB):
                        k = i * (VB * SB) + (u * P + q * SB + n)
                        ins = act.activation(dist[:, n, :], iota[:, :], ACT.Abs, bias=e2s[:, bass.ds(k, 1)], scale=-1.0)
                    ins.then_inc(abs_ready, 1)
                    act.wait_ge(abs_ready, b + 1)
                    act.activation(oh2[:, h, :, :], dist[:, :, :], ACT.Relu, bias=ones[:, 0:1], scale=-1.0).then_inc(oh2_ready, 1)

                def evacuate(b0, u, half, i, q):
                    act.wait_ge(sc_ps, b0 + i * VB + (q + 3))
                    act.activation(W[:, half * HK:(half + 1) * HK, bass.ds(i * (VB * SB) + (u * P + q * SB), SB)],
                                   scat[q % 2][:, 0:SB * HK].rearrange("p (t e) -> p e t", t=SB), ACT.Copy).then_inc(w_evac, 1)

                def quarter(t, b0, u, half, between=None):
                    act.wait_ge(picks_ready, t + 1)
                    hold(act)
                    n = QB // VB
                    for q in range(2):
                        hot(b0, u, 0, q)
                    for lo, hi in ((0, n // 2), (n // 2, n - 1)):
                        with act.Fori(lo, hi) as i:
                            for q in range(VB):
                                evacuate(b0, u, half, i, q)
                                hot(b0, u, i, q + 2)
                        if between is not None and lo == 0:
                            between()
                    for q in range(VB):
                        evacuate(b0, u, half, n - 1, q)
                        if q < 2:
                            hot(b0, u, n - 1, q + 2)

                def gated(g):
                    act.wait_ge(vacc_ready, g + 1)
                    for k in range(KC):
                        ins = act.activation(ev[:, k, :], vacc[:, k, :], ACT.Copy, scale=g2T[:, k, 0:1])
                    ins.then_inc(ev_ready, 1)

                def squares(g):
                    act.wait_ge(x3_ready, g + 1)
                    act.activation(ev[:, :, :], x3[:, :, :], ACT.Square).then_inc(sq4_ready, 1)

                def root(g, n):
                    act.wait_ge(n_ready, g + 1)
                    act.activation(rs4[:, 0:n], nps[:, 0:n], ACT.Sqrt, bias=epsb[:, 0:1], scale=1.0 / D).then_inc(rs_ready, 1)

                def group(g, first, last):
                    quarter(g * 2, batch0(g, 0), 0, 1, None if first else lambda: squares(g - 1))
                    gelu(g * 2 + 2)
                    if not first:
                        root(g - 1, GT)
                    quarter(g * 2 + 1, batch0(g, 1), 1, 1)
                    if not last:
                        quarter(g * 2 + 2, batch0(g, 2), 0, 0)
                        gelu(g * 2 + 3)
                        quarter(g * 2 + 3, batch0(g, 3), 1, 0)
                    gated(g)
                gelu(0)
                quarter(0, 0, 0, 0)
                gelu(1)
                quarter(1, QB, 1, 0)
                group(0, True, False)
                with act.Fori(1, NGRP - 1) as g:
                    group(g, False, False)
                group(NGRP - 1, False, True)
                squares(NGRP - 1)
                root(NGRP - 1, GT)
                act.wait_ge(x3_ready, NGRP + 1)
                act.activation(ev[:, :, 0:TS], x3[:, :, 0:TS], ACT.Square).then_inc(sq4_ready, 1)
                root(NGRP, TS)

            @block.tensor
            def _(pe):
                pe.sem_inc(v_used, VB)

                def turn(t, first=False):
                    pe.wait_ge(ef_ready, t + 1)
                    if not first:
                        pe.wait_ge(picks_ready, t)
                        hold(pe)
                    for w, src in enumerate((dots[:, :], ef[:, 0, :], ef[:, 1, :])):
                        mm = pe.transpose(tps[:, w * P:(w + 1) * P], src, ident[:, :])
                    mm.then_inc(tr4_ready, 1)

                def batch(b, q):
                    h = q % 2
                    pe.wait_ge(oh_ready, b + 1)
                    pe.wait_ge(oh2_ready, b + 2)
                    pe.wait_ge(w_evac, b + 1)
                    for n in range(SB):
                        for j in range(3):
                            mm = pe.matmul(scat[h][:, n * HK:(n + 1) * HK], oh2[:, h, n, :], oh1w[:, h, j, n, :], start=(j == 0), stop=(j == 2), skip_group_check=True)
                    mm.then_inc(sc_ps, 1)

                def quarter(g, q4, scattering, clear):
                    def steps(i, clear):
                        for s in range(VB):
                            pe.wait_ge(v_in[s], g * (16 * NKEY // VB) + i * 16 + (q4 * (16 * QB // VB) + 16))
                            e1 = slice(s, s + 1) if clear else bass.ds(i * VB + (q4 * QB + s), 1)
                            for k in range(KC):
                                mm = pe.matmul(vacc[:, k, :], vbuf[:, s, k * P:(k + 1) * P], W[:, e1, :].rearrange("p o t -> p (o t)"),
                                               start=(clear and s == 0 and k % 2 == 0), stop=False, skip_group_check=True)
                            mm.then_inc(v_used, 1)
                            if scattering:
                                batch(batch0(g, q4) + i * VB + s, s)
                    lo = 0
                    if clear:
                        steps(0, True)
                        lo = 1
                    hold(pe)
                    with pe.Fori(lo, QB // VB) as i:
                        steps(i, False)

                def scatter(b0):
                    with pe.Fori(0, QB // VB) as i:
                        for s in range(VB):
                            batch(i * VB + (b0 + s), s)

                def sums(g, n=GT):
                    pe.wait_ge(sq4_ready, g + 1)
                    for k in range(KC):
                        mm = pe.matmul(nps[:, 0:n], ones[:, :], ev[:, k, 0:n], start=(k == 0), stop=(k == KC - 1))
                    mm.then_inc(n_ready, 1)

                def group(g, first, last):
                    pe.wait_ge(ev_ready, g + 1)
                    pe.wait_ge(w_evac, batch0(g, 0) + 2)
                    quarter(g, 0, True, True)
                    if not first:
                        sums(g - 1)
                    if not last:
                        turn(g * 2 + 2)
                    quarter(g, 1, True, False)
                    pe.wait_ge(w_evac, batch0(g, 2) + 2)
                    quarter(g, 2, not last, False)
                    if not last:
                        turn(g * 2 + 3)
                    quarter(g, 3, not last, False)
                    pe.wait_ge(v_used, g * NKEY + (NKEY + VB))
                    pe.sem_inc(vacc_ready, 1)
                turn(0, True)
                scatter(0)
                turn(1)
                scatter(QB)
                group(0, True, False)
                with pe.Fori(1, NGRP - 1) as g:
                    group(g, False, False)
                group(NGRP - 1, False, True)
                sums(NGRP - 1)
                pe.wait_ge(acc_ready, 1)
                hold(pe)
                for k in range(KC):
                    mm = pe.transpose(tps[:, k * TS:(k + 1) * TS], acc[0:TS, k * P:(k + 1) * P], ident[0:TS, 0:TS])
                mm.then_inc(tr4_ready, 1)
                sums(NGRP, TS)


OUTS = {
    "y": (KC, P, T), "ret_prompt": (H, DK, P), "ret_sample": (NB, H, DK, P),
    "conv": (P, KC, (1 + NB) * HIST), "lru": (P, KC, 1 + NB),
}
SCRATCH = {"mg": (KC, P, T), "x2": (KC, P, T), "hn2": (NT, P, D)}


def kernel(**inputs):
    import concourse.bacc as bacc
    from concourse.bass_utils import run_bass_kernel_spmd as run

    a = {k: np.asarray(v) for k, v in inputs.items()}

    def chunks(x):
        return x.reshape(-1, KC, P).transpose(2, 1, 0)

    x = np.concatenate([a["x_prompt"].reshape(SEQ, D), a["x_sample"].reshape(TS, D)])
    c = np.concatenate([a["c_prompt"], a["c_sample"]])
    w = a["w_in"][0]
    cuts = [w[:, i * 64:(i + 1) * 64] for i in range(16)]
    rest = [[w[:, 1024 + g * 1024 + f * P:1024 + g * 1024 + (f + 1) * P] for f in range(KC)] for g in range(6)]
    v_, g_ret, x_lru, g_lru, gate_a, gate_b = rest
    w_in = np.stack([np.concatenate([cuts[f], cuts[8 + f], v_[f], x_lru[f], g_lru[f], g_ret[f], gate_a[f], gate_b[f]], axis=1) for f in range(KC)])
    vecs = np.concatenate([a["norm1_w"], a["norm2_w"], a["ret_gn_w"], a["conv_b"], a["conv_w"][0], a["lru_ba"], a["lru_bx"], a["lru_lambda"],
                           a["final_norm_w"].reshape(1, D)])
    wax = np.stack([a["lru_wa"][0], a["lru_wx"][0]], axis=2).reshape(KC, P, 2, 64)
    arrays = {
        "xT": x.T, "cT": chunks(c), "w_ada": a["w_ada"][0], "bada": a["b_ada"].reshape(48, P).T,
        "vec": vecs.reshape(NVEC, KC, P).transpose(2, 0, 1), "w_in": w_in, "wax": wax,
        "state_ret": a["state_ret"][0], "h0": chunks(a["state_lru"][0]),
        "c0": a["state_conv"][0].reshape(NB * HIST, KC, P).transpose(2, 1, 0),
        "w_out": a["w_out"][0], "peer_wq": a["peer_wq"][0],
        "keys": np.stack([a["peer_k1"][0].T, a["peer_k2"][0].T], axis=1),
        "peer_u": a["peer_u"][0], "peer_v": a["peer_v"][0],
    }
    arrays = {k: np.ascontiguousarray(v) for k, v in arrays.items()}
    arrays.update(tables())
    nc = bacc.Bacc("TRN2", target_bir_lowering=False, num_devices=1)
    I = {k: nc.dram_tensor(f"in_{k}", v.shape, F32, kind="ExternalInput").ap() for k, v in arrays.items()}
    O = {k: nc.dram_tensor(f"out_{k}", s, F32, kind="ExternalOutput").ap() for k, s in OUTS.items()}
    S = {k: nc.dram_tensor(f"scratch_{k}", s, F32, kind="Internal").ap() for k, s in SCRATCH.items()}
    program(nc, I, O, S)
    r = run(nc, [{f"in_{k}": v for k, v in arrays.items()}], core_ids=[0]).results[0]
    o = {k: r[f"out_{k}"] for k in OUTS}
    conv = o["conv"].reshape(P, KC, 1 + NB, HIST).transpose(2, 3, 1, 0).reshape(1 + NB, HIST, D)
    lru = o["lru"].transpose(2, 1, 0).reshape(1 + NB, D)
    y = o["y"].reshape(D, T).T
    return (y[:SEQ].reshape(1, SEQ, D), y[SEQ:].reshape(NB, NS, D), o["ret_prompt"].reshape(1, 1, H, DK, P),
            lru[None, 0:1], conv[None, 0:1], o["ret_sample"].reshape(1, NB, H, DK, P), lru[None, 1:], conv[None, 1:])
```
